# Optimizing a Trainium2 kernel written in Bass

```python
import jax
import jax.numpy as jnp
from jax import lax
import numpy as np
import math
import jax, jax.numpy as jnp

D_MODEL = 1024
BATCH = 1
SEQ = 256
DEPTH = 1

D_MIX = D_MODEL
RWKV_WIDTH = D_MIX // 2
RWKV_HEAD_DIM = 64
RWKV_HEADS = RWKV_WIDTH // RWKV_HEAD_DIM
DECAY_LORA = 64
ICLR_LORA = 64
GATE_LORA = 128
GLA_V_WIDTH = D_MIX - RWKV_WIDTH
GLA_HEADS = 4
GLA_DV = GLA_V_WIDTH // GLA_HEADS
GLA_DK = GLA_DV // 2
GLA_K_WIDTH = GLA_HEADS * GLA_DK
GLA_GATE_LORA = 16
GLA_TAU = 16.0
GLA_CHUNK = 16
N_GROUPS = 4
EXPERTS_PER_GROUP = 8
N_EXPERTS = N_GROUPS * EXPERTS_PER_GROUP
TOP_K = 2
D_EXPERT = 512
MOE_BLOCK = 128
RMS_EPS = 1e-6
RWKV_GN_EPS = 64e-5

RWKV_SPLITS = (RWKV_WIDTH, RWKV_WIDTH, RWKV_WIDTH, DECAY_LORA, DECAY_LORA, ICLR_LORA, ICLR_LORA, GATE_LORA)
GLA_SPLITS = (GLA_K_WIDTH, GLA_K_WIDTH, GLA_V_WIDTH, GLA_GATE_LORA, GLA_GATE_LORA, GLA_V_WIDTH)
RWKV_COLS = sum(RWKV_SPLITS)
D_IN_PROJ = RWKV_COLS + sum(GLA_SPLITS)


def _split(p, sizes):
    return jnp.split(p, np.cumsum(sizes)[:-1].tolist(), axis=-1)

def rmsnorm(x, w):
    xf = x.astype(jnp.float32)
    y = xf * lax.rsqrt(jnp.mean(xf * xf, axis=-1, keepdims=True) + RMS_EPS)
    return (y * w.astype(jnp.float32)).astype(x.dtype)

def centred_shift(p):
    prev = jnp.pad(p[:, :-1], ((0, 0), (1, 0), (0, 0)))
    nxt = jnp.pad(p[:, 1:], ((0, 0), (0, 1), (0, 0)))
    return 0.5 * (prev + nxt)

def rwkv7_bidir_scan(r, w, k, v, kk, b):
    def to_dir(z):
        z = jnp.stack([z[0], jnp.flip(z[1], axis=1)])
        return jnp.moveaxis(z, 2, 0)

    def both(z):
        return to_dir(jnp.stack([z, z]))

    xs = (both(r), to_dir(w), to_dir(k), both(v), both(kk), to_dir(b))
    bsz, _, h, n = r.shape
    s0 = jnp.zeros((2, bsz, h, n, n), jnp.float32)

    def step(s, inp):
        r_t, w_t, k_t, v_t, kk_t, b_t = inp
        sa = jnp.einsum('dbhvk,dbhk->dbhv', s, -kk_t)
        s = s * w_t[..., None, :] + sa[..., None] * b_t[..., None, :] + v_t[..., None] * k_t[..., None, :]
        return s, jnp.einsum('dbhvk,dbhk->dbhv', s, r_t)

    _, ys = lax.scan(step, s0, xs)
    ys = jnp.moveaxis(ys, 0, 2)
    return ys[0] + jnp.flip(ys[1], axis=1)

def rwkv7_mixer(p, mu, w0_f, w2_f, w0_b, w2_b, a0_f, a2_f, a0_b, a2_b, g2, k_k, k_a, r_k, ln_w, ln_b):
    p = p.astype(jnp.float32)
    p = p + mu * (centred_shift(p) - p)
    r, k, v, wl_f, wl_b, al_f, al_b, gl = _split(p, RWKV_SPLITS)

    def decay(w0, wl, w2):
        logw = -jax.nn.softplus(-(w0 + jnp.tanh(wl) @ w2)) - 0.5
        return jnp.exp(-jnp.exp(logw))

    def heads(z):
        return z.reshape(z.shape[:-1] + (RWKV_HEADS, RWKV_HEAD_DIM))

    w = jnp.stack([decay(w0_f, wl_f, w2_f), decay(w0_b, wl_b, w2_b)])
    a = jax.nn.sigmoid(jnp.stack([a0_f + al_f @ a2_f, a0_b + al_b @ a2_b]))
    g = jax.nn.sigmoid(gl) @ g2
    kk = heads(k * k_k)
    kk = kk / jnp.maximum(jnp.sqrt(jnp.sum(kk * kk, axis=-1, keepdims=True)), 1e-12)
    k_dir = k * (1.0 + (a - 1.0) * k_a)
    b = kk * heads(a)
    rh, vh = heads(r), heads(v)
    y = rwkv7_bidir_scan(rh, heads(w), heads(k_dir), vh, kk, b)
    mean = jnp.mean(y, axis=-1, keepdims=True)
    var = jnp.var(y, axis=-1, keepdims=True)
    y = (y - mean) * lax.rsqrt(var + RWKV_GN_EPS)
    y = y.reshape(y.shape[:-2] + (RWKV_WIDTH,)) * ln_w + ln_b
    bonus = jnp.sum(rh * heads(k_dir[0] + k_dir[1]) * r_k, axis=-1, keepdims=True) * vh
    return (y + bonus.reshape(y.shape)) * g

def gla_chunked(q, k, v, g):
    bsz, h, t, dk = q.shape
    dv = v.shape[-1]
    c = GLA_CHUNK
    n = t // c
    q, k, g = (z.reshape(bsz, h, n, c, dk) for z in (q, k, g))
    v = v.reshape(bsz, h, n, c, dv)
    bc = jnp.cumsum(g, axis=3)
    causal = jnp.tril(jnp.ones((c, c), dtype=bool))
    diff = bc[..., :, None, :] - bc[..., None, :, :]
    dec = jnp.exp(jnp.where(causal[:, :, None], diff, -jnp.inf))
    att = jnp.einsum('bhnid,bhnjd,bhnijd->bhnij', q, k, dec)
    o = jnp.einsum('bhnij,bhnjv->bhniv', att, v)
    b_last = bc[..., -1, :]
    u = jnp.einsum('bhncd,bhncv->nbhdv', k * jnp.exp(b_last[..., None, :] - bc), v)

    def step(s, inp):
        u_n, d_n = inp
        return s * d_n[..., None] + u_n, s

    s0 = jnp.zeros((bsz, h, dk, dv), jnp.float32)
    _, s_in = lax.scan(step, s0, (u, jnp.moveaxis(jnp.exp(b_last), 2, 0)))
    o = o + jnp.einsum('bhncd,nbhdv->bhncv', q * jnp.exp(bc), s_in)
    return o.reshape(bsz, h, t, dv)

def gla_mixer(p, gw2_f, gb_f, gw2_b, gb_b, norm_w):
    p = p.astype(jnp.float32)
    bsz, t, _ = p.shape
    q, k, v, gl_f, gl_b, og = _split(p, GLA_SPLITS)

    def heads(z, d):
        return jnp.moveaxis(z.reshape(z.shape[:-1] + (GLA_HEADS, d)), 2, 1)

    q = heads(q, GLA_DK) * (GLA_DK ** -0.5)
    k = heads(k, GLA_DK)
    v = heads(v, GLA_DV)
    g_f = heads(jax.nn.log_sigmoid(gl_f @ gw2_f + gb_f) / GLA_TAU, GLA_DK)
    g_b = heads(jax.nn.log_sigmoid(gl_b @ gw2_b + gb_b) / GLA_TAU, GLA_DK)

    def flip(z):
        return jnp.flip(z, axis=2)

    o = gla_chunked(q, k, v, g_f) + flip(gla_chunked(flip(q), flip(k), flip(v), flip(g_b)))
    o = o * lax.rsqrt(jnp.mean(o * o, axis=-1, keepdims=True) + RMS_EPS)
    o = jnp.moveaxis(o, 1, 2).reshape(bsz, t, GLA_V_WIDTH)
    return o * norm_w * jax.nn.silu(og)

def hier_moe(h, w_coarse, b_coarse, w_fine, b_fine, w_gate, w_up, w_down):
    bsz, t, d = h.shape
    n_tok = bsz * t
    hf = h.reshape(n_tok, d)
    tok_idx = jnp.arange(n_tok)
    coarse = (hf @ w_coarse + b_coarse).astype(jnp.float32)
    pc = jax.nn.softmax(coarse, axis=-1)
    gsel = jnp.argmax(coarse, axis=-1)
    pg = pc[tok_idx, gsel]
    fine = (hf @ w_fine + b_fine).astype(jnp.float32).reshape(n_tok, N_GROUPS, EXPERTS_PER_GROUP)
    pf = jax.nn.softmax(fine[tok_idx, gsel], axis=-1)
    top_p, top_e = lax.top_k(pf, TOP_K)
    comb = pg[:, None] * top_p / jnp.sum(top_p, axis=-1, keepdims=True)
    eid = (gsel[:, None] * EXPERTS_PER_GROUP + top_e).reshape(-1).astype(jnp.int32)
    n_asg = n_tok * TOP_K
    tok = jnp.repeat(tok_idx, TOP_K).astype(jnp.int32)
    wts = comb.reshape(-1)
    order = jnp.argsort(eid, stable=True)
    se, st, sw = eid[order], tok[order], wts[order]
    counts = jnp.bincount(eid, length=N_EXPERTS).astype(jnp.int32)
    starts = jnp.cumsum(counts) - counts
    padded = ((counts + MOE_BLOCK - 1) // MOE_BLOCK) * MOE_BLOCK
    pends = jnp.cumsum(padded)
    pstarts = pends - padded
    dest = pstarts[se] + jnp.arange(n_asg, dtype=jnp.int32) - starts[se]
    n_blocks = -(-n_asg // MOE_BLOCK) + N_EXPERTS
    n_rows = n_blocks * MOE_BLOCK
    row_tok = jnp.zeros((n_rows,), jnp.int32).at[dest].set(st)
    row_w = jnp.zeros((n_rows,), jnp.float32).at[dest].set(sw)
    block_e = jnp.minimum(jnp.searchsorted(pends, jnp.arange(n_blocks, dtype=jnp.int32) * MOE_BLOCK, side='right'), N_EXPERTS - 1)
    xs = hf[row_tok].reshape(n_blocks, MOE_BLOCK, d)

    def expert_block(args):
        xb, e = args
        return (jax.nn.silu(xb @ w_gate[e]) * (xb @ w_up[e])) @ w_down[e]

    ys = lax.map(expert_block, (xs, block_e)).reshape(n_rows, d)
    out = jax.ops.segment_sum(ys * row_w[:, None].astype(ys.dtype), row_tok, num_segments=n_tok)
    return out.reshape(bsz, t, d)

def first_inputs(seed: int = 0) -> dict:
    key = jax.random.key(seed)
    ks = iter(jax.random.split(key, 40))

    def nrm(shape, scale):
        return jax.random.normal(next(ks), shape, jnp.float32) * scale

    def unif(shape, lo, hi):
        return jax.random.uniform(next(ks), shape, jnp.float32, lo, hi)

    L, D = DEPTH, D_MODEL
    return {
        'x': nrm((BATCH, SEQ, D), 1.0),
        'ln1_w': 1.0 + nrm((L, D), 0.05),
        'w_in': nrm((L, D, D_IN_PROJ), D ** -0.5),
        'rw_mu': unif((L, RWKV_COLS), 0.0, 1.0),
        'rw_w0_f': unif((L, RWKV_WIDTH), -6.0, -1.0),
        'rw_w2_f': nrm((L, DECAY_LORA, RWKV_WIDTH), 0.1),
        'rw_w0_b': unif((L, RWKV_WIDTH), -6.0, -1.0),
        'rw_w2_b': nrm((L, DECAY_LORA, RWKV_WIDTH), 0.1),
        'rw_a0_f': nrm((L, RWKV_WIDTH), 0.1),
        'rw_a2_f': nrm((L, ICLR_LORA, RWKV_WIDTH), 0.5 * ICLR_LORA ** -0.5),
        'rw_a0_b': nrm((L, RWKV_WIDTH), 0.1),
        'rw_a2_b': nrm((L, ICLR_LORA, RWKV_WIDTH), 0.5 * ICLR_LORA ** -0.5),
        'rw_g2': nrm((L, GATE_LORA, RWKV_WIDTH), GATE_LORA ** -0.5),
        'rw_k_k': 0.85 + nrm((L, RWKV_WIDTH), 0.05),
        'rw_k_a': 1.0 + nrm((L, RWKV_WIDTH), 0.05),
        'rw_r_k': nrm((L, RWKV_HEADS, RWKV_HEAD_DIM), 0.1),
        'rw_ln_w': 1.0 + nrm((L, RWKV_WIDTH), 0.05),
        'rw_ln_b': nrm((L, RWKV_WIDTH), 0.01),
        'gla_gw2_f': nrm((L, GLA_GATE_LORA, GLA_K_WIDTH), GLA_GATE_LORA ** -0.5),
        'gla_gb_f': 2.0 + nrm((L, GLA_K_WIDTH), 0.5),
        'gla_gw2_b': nrm((L, GLA_GATE_LORA, GLA_K_WIDTH), GLA_GATE_LORA ** -0.5),
        'gla_gb_b': 2.0 + nrm((L, GLA_K_WIDTH), 0.5),
        'gla_norm_w': 1.0 + nrm((L, GLA_V_WIDTH), 0.05),
        'w_out': nrm((L, D_MIX, D), D_MIX ** -0.5),
        'ln2_w': 1.0 + nrm((L, D), 0.05),
        'moe_w_coarse': nrm((L, D, N_GROUPS), D ** -0.5),
        'moe_b_coarse': nrm((L, N_GROUPS), 0.01),
        'moe_w_fine': nrm((L, D, N_EXPERTS), D ** -0.5),
        'moe_b_fine': nrm((L, N_EXPERTS), 0.01),
        'moe_w_gate': nrm((L, N_EXPERTS, D, D_EXPERT), D ** -0.5),
        'moe_w_up': nrm((L, N_EXPERTS, D, D_EXPERT), D ** -0.5),
        'moe_w_down': nrm((L, N_EXPERTS, D_EXPERT, D), D_EXPERT ** -0.5),
        'ln_f_w': 1.0 + nrm((D,), 0.05),
    }

def first_block(x, ln1_w, w_in, rw_mu, rw_w0_f, rw_w2_f, rw_w0_b, rw_w2_b, rw_a0_f, rw_a2_f, rw_a0_b, rw_a2_b, rw_g2, rw_k_k, rw_k_a, rw_r_k, rw_ln_w, rw_ln_b, gla_gw2_f, gla_gb_f, gla_gw2_b, gla_gb_b, gla_norm_w, w_out, ln2_w, moe_w_coarse, moe_b_coarse, moe_w_fine, moe_b_fine, moe_w_gate, moe_w_up, moe_w_down, ln_f_w):
    for l in range(DEPTH):
        h = rmsnorm(x, ln1_w[l])
        p = h @ w_in[l]
        y_rw = rwkv7_mixer(p[..., :RWKV_COLS], rw_mu[l], rw_w0_f[l], rw_w2_f[l], rw_w0_b[l], rw_w2_b[l],
                           rw_a0_f[l], rw_a2_f[l], rw_a0_b[l], rw_a2_b[l], rw_g2[l], rw_k_k[l], rw_k_a[l],
                           rw_r_k[l], rw_ln_w[l], rw_ln_b[l])
        y_gla = gla_mixer(p[..., RWKV_COLS:], gla_gw2_f[l], gla_gb_f[l], gla_gw2_b[l], gla_gb_b[l], gla_norm_w[l])
        mix = jnp.concatenate([y_rw, y_gla], axis=-1).astype(x.dtype)
        x = x + mix @ w_out[l]
        x = x + hier_moe(rmsnorm(x, ln2_w[l]), moe_w_coarse[l], moe_b_coarse[l], moe_w_fine[l], moe_b_fine[l],
                         moe_w_gate[l], moe_w_up[l], moe_w_down[l])
    return rmsnorm(x, ln_f_w)


DEPTH_2 = 2

GRID_W = 64
CTX_LEN = 256
HEAD_DIM = 64
A_HEADS = 8
A_KV_HEADS = 2
A_GROUP = A_HEADS // A_KV_HEADS
B_HEADS = 4
B_V_DIM = 2 * HEAD_DIM
C_GROUPS = 4
C_GROUP_DIM = 128
N_BRANCH = 3
BRANCH_W = 512
A_Q_W = A_HEADS * HEAD_DIM
A_KV_W = A_KV_HEADS * HEAD_DIM
B_QK_W = B_HEADS * 2 * HEAD_DIM
B_V_W = B_HEADS * B_V_DIM
C_W = C_GROUPS * C_GROUP_DIM
GATE_W = N_BRANCH * D_MODEL
IN_W = A_Q_W + 2 * A_KV_W + 2 * B_QK_W + B_V_W + C_W + GATE_W
D_FF = ((8 * D_MODEL // 3 + 127) // 128) * 128
N_MOD = 9
Q_BLOCK = 128
ROPE_THETA = 10000.0
EPS = 1e-6


def rmsnorm_2(x, g):
    xf = x.astype(jnp.float32)
    y = xf * lax.rsqrt(jnp.mean(xf * xf, axis=-1, keepdims=True) + EPS)
    return (y * g.astype(jnp.float32)).astype(x.dtype)

def modulate(x, shift, scale):
    return x * (1 + scale[:, None, :]) + shift[:, None, :]

def swiglu(x, wi, wo):
    g, u = jnp.split(x @ wi, 2, axis=-1)
    return (jax.nn.silu(g) * u) @ wo

def ffn_half(h, m, k, g_norm, wi, wo):
    hn = modulate(rmsnorm_2(h, g_norm), m[3 * k], m[3 * k + 1])
    return h + 0.5 * m[3 * k + 2][:, None, :] * swiglu(hn, wi, wo)

def axial_rope(n_tok):
    rows = n_tok // GRID_W
    row = jnp.repeat(jnp.arange(rows, dtype=jnp.float32), GRID_W)
    col = jnp.tile(jnp.arange(GRID_W, dtype=jnp.float32), rows)
    n_freq = HEAD_DIM // 4
    inv = jnp.power(ROPE_THETA, -jnp.arange(n_freq, dtype=jnp.float32) / n_freq)
    ang = jnp.concatenate([row[:, None] * inv, col[:, None] * inv], axis=-1)
    return jnp.cos(ang), jnp.sin(ang)

def apply_rope(x, cos, sin):
    shp = (1, x.shape[1]) + (1,) * (x.ndim - 3) + (x.shape[-1] // 2,)
    cs = cos.reshape(shp).astype(x.dtype)
    sn = sin.reshape(shp).astype(x.dtype)
    x1, x2 = jnp.split(x, 2, axis=-1)
    return jnp.concatenate([x1 * cs - x2 * sn, x1 * sn + x2 * cs], axis=-1)

def split_projection(z):
    sizes = (A_Q_W, A_KV_W, A_KV_W, B_QK_W, B_QK_W, B_V_W, C_W)
    idx = []
    o = 0
    for s in sizes:
        o += s
        idx.append(o)
    return jnp.split(z, idx, axis=-1)

def project_tokens(hn, w_in, qk_g, cos, sin):
    bn, n = hn.shape[:2]
    qa, ka, va, qb, kb, vb, uc, gl = split_projection(hn @ w_in)
    qa = rmsnorm_2(qa.reshape(bn, n, A_KV_HEADS, A_GROUP, HEAD_DIM), qk_g[0])
    ka = rmsnorm_2(ka.reshape(bn, n, A_KV_HEADS, HEAD_DIM), qk_g[1])
    va = va.reshape(bn, n, A_KV_HEADS, HEAD_DIM)
    qb = rmsnorm_2(qb.reshape(bn, n, B_HEADS, 2, HEAD_DIM), qk_g[2])
    kb = rmsnorm_2(kb.reshape(bn, n, B_HEADS, 2, HEAD_DIM), qk_g[3])
    vb = vb.reshape(bn, n, B_HEADS, B_V_DIM)
    if cos is not None:
        qa = apply_rope(qa, cos, sin)
        ka = apply_rope(ka, cos, sin)
        qb = apply_rope(qb, cos, sin)
        kb = apply_rope(kb, cos, sin)
    uc = uc.reshape(bn, n, C_GROUPS, C_GROUP_DIM)
    return qa, ka, va, qb, kb, vb, uc, gl

def gqa_attend(q, k, v):
    s = jnp.einsum('bqhgd,bkhd->bhgqk', q.astype(jnp.float32) * HEAD_DIM ** -0.5, k.astype(jnp.float32))
    p = jax.nn.softmax(s, axis=-1)
    return jnp.einsum('bhgqk,bkhd->bqhgd', p.astype(v.dtype), v)

def diff_attend(q, k, v, lam):
    s = jnp.einsum('bqhmd,bkhmd->bhmqk', q.astype(jnp.float32) * HEAD_DIM ** -0.5, k.astype(jnp.float32))
    p = jax.nn.softmax(s, axis=-1)
    p = p[:, :, 0] - lam * p[:, :, 1]
    return jnp.einsum('bhqk,bkhe->bqhe', p.astype(v.dtype), v)

def sweep_query_blocks(fn, q):
    bn, s = q.shape[:2]
    nb = s // Q_BLOCK
    blocks = jnp.moveaxis(q.reshape((bn, nb, Q_BLOCK) + q.shape[2:]), 1, 0)
    out = jnp.moveaxis(lax.map(fn, blocks), 0, 1)
    return out.reshape((bn, s) + out.shape[3:])

def diff_lambda(lp, lam_init):
    lpf = lp.astype(jnp.float32)
    return jnp.exp(jnp.sum(lpf[0] * lpf[1])) - jnp.exp(jnp.sum(lpf[2] * lpf[3])) + lam_init

def fourier_mix(u):
    f = jnp.fft.fft2(u.astype(jnp.float32), axes=(1, 3), norm='ortho')
    return jnp.real(f).astype(u.dtype)

def merge_branches(ya, yb, yc, gl, w_branch, w_out):
    bn, n = ya.shape[:2]
    br = jnp.stack([ya.reshape(bn, n, BRANCH_W), yb.reshape(bn, n, BRANCH_W), yc.reshape(bn, n, BRANCH_W)], axis=2)
    proj = jnp.einsum('bnie,ied->bnid', br, w_branch)
    gates = jax.nn.sigmoid(gl.reshape(bn, n, N_BRANCH, D_MODEL))
    return jnp.sum(gates * proj, axis=2) @ w_out

def second_inputs(seed: int = 0) -> dict:
    key = jax.random.key(seed)
    ks = jax.random.split(key, 16)
    f32 = jnp.float32
    d = D_MODEL
    x = jax.random.normal(ks[0], (BATCH, SEQ, d), f32)
    c = jax.random.normal(ks[1], (BATCH, d), f32)
    ctx = jax.random.normal(ks[2], (BATCH, CTX_LEN, d), f32)
    c_ctx = jax.random.normal(ks[3], (d,), f32)
    w_ada = jax.random.normal(ks[4], (DEPTH_2, d, N_MOD * d), f32) * (0.5 * d ** -0.5)
    b_ada = jax.random.normal(ks[5], (DEPTH_2, N_MOD * d), f32) * 0.02
    norm_g = 1.0 + 0.05 * jax.random.normal(ks[6], (DEPTH_2, 3, d), f32)
    ffn_wi = jax.random.normal(ks[7], (DEPTH_2, 2, d, 2 * D_FF), f32) * d ** -0.5
    ffn_wo = jax.random.normal(ks[8], (DEPTH_2, 2, D_FF, d), f32) * D_FF ** -0.5
    w_in = jax.random.normal(ks[9], (DEPTH_2, d, IN_W), f32) * d ** -0.5
    qk_g = 1.0 + 0.05 * jax.random.normal(ks[10], (DEPTH_2, 4, HEAD_DIM), f32)
    diff_lam = 0.1 * jax.random.normal(ks[11], (DEPTH_2, 4, HEAD_DIM), f32)
    diff_subln_g = 1.0 + 0.05 * jax.random.normal(ks[12], (DEPTH_2, B_V_DIM), f32)
    w_branch = jax.random.normal(ks[13], (DEPTH_2, N_BRANCH, BRANCH_W, d), f32) * BRANCH_W ** -0.5
    w_out = jax.random.normal(ks[14], (DEPTH_2, d, d), f32) * d ** -0.5
    return {"x": x, "c": c, "ctx": ctx, "c_ctx": c_ctx, "w_ada": w_ada, "b_ada": b_ada,
            "norm_g": norm_g, "ffn_wi": ffn_wi, "ffn_wo": ffn_wo, "w_in": w_in, "qk_g": qk_g,
            "diff_lam": diff_lam, "diff_subln_g": diff_subln_g, "w_branch": w_branch, "w_out": w_out}

def second_block(x, c, ctx, c_ctx, w_ada, b_ada, norm_g, ffn_wi, ffn_wo, w_in, qk_g,
              diff_lam, diff_subln_g, w_branch, w_out):
    cos, sin = axial_rope(x.shape[1])
    h, hc = x, ctx
    for l in range(DEPTH_2):
        last = l == DEPTH_2 - 1
        ml = jnp.split(jax.nn.silu(c) @ w_ada[l] + b_ada[l], N_MOD, axis=-1)
        mc = jnp.split(jax.nn.silu(c_ctx)[None] @ w_ada[l] + b_ada[l], N_MOD, axis=-1)

        h = ffn_half(h, ml, 0, norm_g[l, 0], ffn_wi[l, 0], ffn_wo[l, 0])
        hc = ffn_half(hc, mc, 0, norm_g[l, 0], ffn_wi[l, 0], ffn_wo[l, 0])

        hn = modulate(rmsnorm_2(h, norm_g[l, 1]), ml[3], ml[4])
        hcn = modulate(rmsnorm_2(hc, norm_g[l, 1]), mc[3], mc[4])
        qa, ka, va, qb, kb, vb, uc, gl = project_tokens(hn, w_in[l], qk_g[l], cos, sin)
        qa_c, ka_c, va_c, qb_c, kb_c, vb_c, uc_c, gl_c = project_tokens(hcn, w_in[l], qk_g[l], None, None)
        lam_init = 0.8 - 0.6 * math.exp(-0.3 * l)
        lam = diff_lambda(diff_lam[l], lam_init)

        ka_all = jnp.concatenate([ka_c, ka], axis=1)
        va_all = jnp.concatenate([va_c, va], axis=1)
        kb_all = jnp.concatenate([kb_c, kb], axis=1)
        vb_all = jnp.concatenate([vb_c, vb], axis=1)
        ya = sweep_query_blocks(lambda qblk: gqa_attend(qblk, ka_all, va_all), qa)
        yb = sweep_query_blocks(lambda qblk: diff_attend(qblk, kb_all, vb_all, lam), qb)
        yb = rmsnorm_2(yb, diff_subln_g[l]) * (1.0 - lam_init)
        yc = fourier_mix(uc)
        h = h + ml[5][:, None, :] * merge_branches(ya, yb, yc, gl, w_branch[l], w_out[l])

        if not last:
            ya_c = gqa_attend(qa_c, ka_c, va_c)
            yb_c = rmsnorm_2(diff_attend(qb_c, kb_c, vb_c, lam), diff_subln_g[l]) * (1.0 - lam_init)
            yc_c = fourier_mix(uc_c)
            hc = hc + mc[5][:, None, :] * merge_branches(ya_c, yb_c, yc_c, gl_c, w_branch[l], w_out[l])

        h = ffn_half(h, ml, 2, norm_g[l, 2], ffn_wi[l, 1], ffn_wo[l, 1])
        if not last:
            hc = ffn_half(hc, mc, 2, norm_g[l, 2], ffn_wi[l, 1], ffn_wo[l, 1])
    return h


def setup_inputs(seed=0):
    out = dict(first_inputs(seed))
    for name, value in second_inputs(seed + 1).items():
        if name != "x":
            out[name + "_2"] = value
    return out


def reference(
    x, ln1_w, w_in, rw_mu, rw_w0_f, rw_w2_f, rw_w0_b, rw_w2_b, rw_a0_f, rw_a2_f, rw_a0_b,
    rw_a2_b, rw_g2, rw_k_k, rw_k_a, rw_r_k, rw_ln_w, rw_ln_b, gla_gw2_f, gla_gb_f, gla_gw2_b,
    gla_gb_b, gla_norm_w, w_out, ln2_w, moe_w_coarse, moe_b_coarse, moe_w_fine, moe_b_fine,
    moe_w_gate, moe_w_up, moe_w_down, ln_f_w, c_2, ctx_2, c_ctx_2, w_ada_2, b_ada_2, norm_g_2,
    ffn_wi_2, ffn_wo_2, w_in_2, qk_g_2, diff_lam_2, diff_subln_g_2, w_branch_2, w_out_2,
):
    x = first_block(
        x, ln1_w, w_in, rw_mu, rw_w0_f, rw_w2_f, rw_w0_b, rw_w2_b, rw_a0_f, rw_a2_f, rw_a0_b,
        rw_a2_b, rw_g2, rw_k_k, rw_k_a, rw_r_k, rw_ln_w, rw_ln_b, gla_gw2_f, gla_gb_f,
        gla_gw2_b, gla_gb_b, gla_norm_w, w_out, ln2_w, moe_w_coarse, moe_b_coarse, moe_w_fine,
        moe_b_fine, moe_w_gate, moe_w_up, moe_w_down, ln_f_w,
    )
    return second_block(
        x, c_2, ctx_2, c_ctx_2, w_ada_2, b_ada_2, norm_g_2, ffn_wi_2, ffn_wo_2, w_in_2, qk_g_2,
        diff_lam_2, diff_subln_g_2, w_branch_2, w_out_2,
    )


_drawn_inputs = setup_inputs


def setup_inputs(seed=0):
    import zlib

    import numpy as np

    out = dict(_drawn_inputs(seed))
    spreads = {}
    factors = {'rw_w2_f': 2.878,
     'rw_w2_b': 5.372,
     'rw_a0_b': 3.223,
     'rw_k_k': 2.775,
     'rw_ln_b': 8.0,
     'moe_b_coarse': 5.755,
     'moe_b_fine': 4.007,
     'norm_g_2': 2.901,
     'qk_g_2': 8.0,
     'diff_lam_2': 5.869,
     'diff_subln_g_2': 6.459}
    for name, (base, spread) in spreads.items():
        noise = np.random.default_rng([zlib.crc32(name.encode()), seed]).standard_normal(out[name].shape)
        drawn = base * np.exp(spread * noise) if base else spread * noise
        out[name] = jnp.asarray(drawn.astype(out[name].dtype))
    for name, factor in factors.items():
        out[name] = (out[name] * factor).astype(out[name].dtype)
    return out
```

```python
from contextlib import ExitStack
import math

import numpy as np

import concourse.bass as bass
from concourse import mybir

F32 = mybir.dt.float32
F32R = mybir.dt.float32r
BF16 = mybir.dt.bfloat16
U16 = mybir.dt.uint16
ACT = mybir.ActivationFunctionType
ALU = mybir.AluOpType
AX_X = mybir.AxisListType.X

P = 128
D = 1024
KT = D // P
TX = 256
T2 = 2 * TX
RW = 512
NCH = RW // P
HD = 64
NG = 4
EPG = 8
NE = NG * EPG
DE = 512
DFF = 2816
NMOD = 9
RMS_EPS = 1e-6
GN_EPS = 64e-5
KAPPA = math.exp(-0.5)
TAU = 16.0

SLAB = 2048
NSLOT = 9
FB = 256
FT = FB // P
S_WIN = 0
N_WIN = 14
S_ADA = S_WIN + N_WIN
N_ADA = 2 * NMOD * D // FB
S_WOUT = S_ADA + N_ADA
S_MOE = S_WOUT + 4
B_MOE = NE * DE // FB
S_LAYER = S_MOE + 3 * B_MOE
B_FFN = DFF // FB
L_FFN0 = 0
L_WIN = 3 * B_FFN
L_MERGE = L_WIN + 11
L_WOUT = L_MERGE + 18
L_FFN1 = L_WOUT + 4
N_LAYER = L_FFN1 + 3 * B_FFN
NSLABS = S_LAYER + 2 * N_LAYER

SMALL = [("ln1", 8), ("mu", 15), ("w0", 8), ("a0", 8), ("kk", 4), ("ka", 4), ("rk", 4), ("lnw", 4),
         ("lnb", 4), ("gb", 4), ("gn", 4), ("ln2", 8), ("lnf", 8), ("rb", 36), ("ng", 48), ("qkg", 8),
         ("sub", 2), ("lam", 8), ("bada", 144), ("c", 16), ("eps", 3)]
MIXP = [("router", 288), ("w2", 512), ("a2", 512), ("g2", 512), ("gw2", 256)]
ATTC = [("cs", 1024), ("c128", 128), ("s128", 128), ("cos", 256), ("sin", 256)]
KEEPC = [("ident", 128), ("o1024", 128), ("o128", 128), ("bo64", 128), ("rot", 128)]
MASKC = [("mask4", 1024), ("level", 1792), ("reset", 1024)]

ADA_KK, ADA_PREP, ADA_MAT, ADA_GLA, ADA_GMAT = 4, 12, 1, 8, 8


def places(layout):
    at, out = 0, {}
    for name, n in layout:
        out[name] = (at, n)
        at += n
    return out, at


def build(nc, slabs, xT, ctxT, small, mixp, attc, keepc, maskc, out):
    SM, NSM = places(SMALL)
    MP, NMP = places(MIXP)
    CA, NCA = places(ATTC)
    CK, NCK = places(KEEPC)
    CM, NCM = places(MASKC)
    ctx = ExitStack()
    with ctx:
        def sb(name, n):
            return ctx.enter_context(nc.sbuf_tensor(name, [P, n], F32))

        ring_at = -(-nc.sbuf_base // 32) * 32
        ring = sb("ring", NSLOT * SLAB)
        keep = sb("keep", NCK)
        par = sb("par", NSM)
        cst = sb("cst", 1920)
        mods = sb("mods", 288)
        xt_ = sb("xt", KT * T2)
        ht_at = -(-nc.sbuf_base // 32) * 32
        ht_ = sb("ht", KT * T2)
        ac_ = sb("ac", KT * T2)
        rs = sb("rs", T2)
        tiny = sb("tiny", 100)
        wk_at = -(-nc.sbuf_base // 32) * 32
        wk = sb("wk", 18432)

        def over(name, base, first, n):
            return nc.alloc_sbuf_tensor_at(name, [P, n], F32R, offset=base + 4 * first)

        wlo = over("wlo", ring_at, 0, NSLOT * SLAB)
        hlo = over("hlo", ht_at, 0, KT * T2)
        hhi = over("hhi", wk_at, 0, KT * T2)
        fhl = over("fhl", wk_at, KT * T2, 3 * 2 * FT * T2)
        W_WHI = KT * T2 + 3 * 2 * FT * T2
        whi = over("whi", wk_at, W_WHI, 3 * SLAB)
        W_FS = W_WHI + 3 * SLAB
        bank = [ctx.enter_context(nc.psum_tensor(f"bank{i}", [P, 512], F32)) for i in range(8)]

        def v3(t, off, a, b):
            return t[:, off:off + a * b].rearrange("p (a b) -> p a b", b=b)

        def v4(t, off, a, b, c):
            return t[:, off:off + a * b * c].rearrange("p (a b c) -> p a b c", b=b, c=c)

        def v5(t, off, a, b, c, d):
            return t[:, off:off + a * b * c * d].rearrange("p (a b c d) -> p a b c d", b=b, c=c, d=d)

        XT = v3(xt_, 0, KT, T2)
        HT = v3(ht_, 0, KT, T2)
        AC = v3(ac_, 0, KT, T2)
        MOD = v4(mods, 0, 2, 72, 2)
        IDENT = keep[:, CK["ident"][0]:CK["ident"][0] + P]
        O1024 = keep[:, CK["o1024"][0]:CK["o1024"][0] + P]
        O128 = keep[:, CK["o128"][0]:CK["o128"][0] + P]
        BO64 = keep[:, CK["bo64"][0]:CK["bo64"][0] + P]
        ROT = keep[:, CK["rot"][0]:CK["rot"][0] + P]

        def pc(name, i=0, n=1):
            o = SM[name][0] + i
            return par[:, o:o + n]

        def b3(b, a=None):
            return bank[b][:, :].rearrange("p (a b) -> p a b", a=a)

        def mp(name):
            return wk[:, MP[name][0]:MP[name][0] + MP[name][1]]

        W_P = NMP
        PT_ = v3(wk, W_P, 20, TX)
        W_KK = W_P + 20 * TX
        KK = v3(wk, W_KK, 4, TX)
        W_KR = W_KK + 1024
        KR = v5(wk, W_KR, 4, 2, 2, P)
        W_BT = W_KR + 2048
        BT = v3(wk, W_BT, 4, TX)
        W_KH = W_BT + 1024
        KH = v3(wk, W_KH, 4, TX)
        W_VT = W_KH + 1024
        VT = v3(wk, W_VT, 2, RW)
        W_Y = W_VT + 1024
        YT = v3(wk, W_Y, 4, TX)
        W_KDS = W_Y + 1024
        KDS = v3(wk, W_KDS, 4, TX)
        W_TAIL = W_KDS + 1024
        W1 = wk[:, W_TAIL:W_TAIL + 512]
        SA = wk[:, W_TAIL + 512:W_TAIL + 1024]
        ST = v3(wk, W_TAIL + 1024, 4, HD)
        BTK = wk[:, W_TAIL + 1280:W_TAIL + 1792]
        KHK = wk[:, W_TAIL + 1792:W_TAIL + 2304]
        MT = v3(ac_, 0, 8, 512)
        TI = [v3(ht_, 512 * g, 4, P) for g in range(2)]
        TTI = [v3(ht_, 1024 + 512 * g, 4, P) for g in range(2)]
        X1 = [v3(ht_, 2048 + 512 * g, 4, P) for g in range(2)]
        AO = [v3(ht_, 3072 + 512 * g, 4, P) for g in range(2)]
        SG_, C_, CI_, CX_ = (v3(ac_, 1024 * i, 4, TX) for i in range(4))
        E2_ = v3(ht_, 0, 4, TX)
        CR = tiny[:, 0:4]
        OMKA = tiny[:, 4:8]
        NCST = NCM // 2
        cbf = cst[:, 0:NCST].bitcast(BF16)
        MASK4 = cbf[:, CM["mask4"][0]:CM["mask4"][0] + 1024].rearrange("p (d n) -> p d n", d=2)
        LEVEL = cbf[:, CM["level"][0]:CM["level"][0] + 1792].rearrange("p (d l n) -> p d l n", d=2, l=7)
        RESET = cbf[:, CM["reset"][0]:CM["reset"][0] + 1024]
        def p_tile(i):
            return PT_[:, i, :] if i < 20 else XT[:, i - 20, TX:T2]
        GV = XT[:, 0:4, TX:T2]
        GOG = XT[:, 4:8, TX:T2]
        U_, AB_, GC_, GCI_ = (v3(ac_, 1024 * i, 4, TX) for i in range(4))
        GE1, GE3 = (v3(ht_, 1024 * i, 4, TX) for i in range(2))
        QH = v3(wk, W_KR, 4, TX)
        KG = v3(wk, W_KR + 1024, 4, TX)
        DT = v5(wk, W_BT, 2, 2, 4, P)
        OT = v3(wk, W_VT, 4, TX)
        VG = v3(wk, W_TAIL, 2, 512)
        KGT = v4(wk, W_TAIL + 1024, 2, 2, P)
        STG = v4(wk, W_TAIL + 1536, 2, 2, P)
        CRG = tiny[:, 8:12]
        CEN, SQM, RSM, TB = (v3(ac_, 1024 * i, 4, TX) for i in range(4))
        MIX = v3(ht_, 0, 8, TX)
        SIL = v3(ht_, 2048, 4, TX)
        RSG = v3(ht_, 3072, 4, TX)
        W_R = 8192
        LG = v3(wk, W_R, 2, 36)
        RT = [v3(wk, W_R + 128 + 64 * i, 2, NE) for i in range(8)]
        RC = [v3(wk, W_R + 700 + 8 * i, 2, NG) for i in range(4)]
        R1 = [wk[:, W_R + 760 + 2 * i:W_R + 762 + 2 * i] for i in range(8)]
        COMB = v3(rs, 0, 2, NE)
        HHI = v3(hhi, 0, KT, T2)
        HLO = v3(hlo, 0, KT, T2)
        FHI = [v3(fhl, 2 * FT * T2 * i, FT, T2) for i in range(3)]
        FLO = [v3(fhl, 2 * FT * T2 * i + FT * T2, FT, T2) for i in range(3)]
        FS = [wk[:, W_FS + T2 * i:W_FS + T2 * (i + 1)] for i in range(2)]
        CBS = [wk[:, W_FS + 2 * T2 + TX * i:W_FS + 2 * T2 + TX * (i + 1)] for i in range(3)]
        DG = v3(wk, W_FS + 2 * T2 + 3 * TX, 2, P)
        QK = v3(wk, 0, 13, T2)
        VA = v3(wk, 6656, 4, P)
        VB = v3(wk, 7168, 4, 512)
        UC = v3(wk, 9216, 4, 512)
        YC = v3(wk, 11264, 4, T2)
        SQ = [wk[:, 13312 + 512 * i:13824 + 512 * i] for i in range(2)]
        RQ = [wk[:, 14336 + 512 * i:14848 + 512 * i] for i in range(2)]
        RTMP = [wk[:, 15360 + TX * i:15360 + TX * (i + 1)] for i in range(2)]
        FTM = [wk[:, 16128 + 512 * i:16640 + 512 * i] for i in range(2)]
        PR = [[ac_[:, 1024 * q + 512 * m:1024 * q + 512 * m + 512] for m in range(2)] for q in range(2)]
        PTR = [[v3(ac_, 2048 + 1024 * q + 512 * m, 4, P) for m in range(2)] for q in range(2)]
        GS = [QK[:, 9 + i, :] for i in range(2)]
        GTMP = [QK[:, 11 + i, :] for i in range(2)]
        ca = {n: cst[:, o:o + k] for n, (o, k) in CA.items()}
        CS = ca["cs"].rearrange("p (a b) -> p a b", a=2)
        AMOD = v3(tiny, 16, 8, 2)
        GMOD = v3(tiny, 32, 8, 2)
        NM = tiny[:, 48:52]
        RSUM = tiny[:, 52:56]
        RREC = tiny[:, 56:60]
        LAMV = tiny[:, 60:64]
        LAME = tiny[:, 64:66]
        NLAM = tiny[:, 66:67]
        SUBS = tiny[:, 68:69]
        CSIL = v3(tiny, 72, 8, 2)
        SROW = [wk[:, W_TAIL - 0 + 2304 - 0 + 256 * i:W_TAIL + 2304 + 256 * (i + 1)] for i in range(2)]

        sems = {}

        def sem(name):
            return sems[name]

        for name in (
            "consts xin ctxin attin sq ss sd hs hn xr slab_used proj projc shifted lin lora sig vtr vtrc cpre exps "
            "prep kk kks kk2 kkq kkd ktr ktrc mat matc w1 w1c sa sac yb ybc stp stc "
            "gu_ gu2 gln gpre gexp gprep gtr gtrc gmat gmatc gst gstc go goc ym ymc ysq yv yvd ybon ybc2 yg gsq gss "
            "gssd gsil mixr wo silc adm adr adt modc lam lamd lame lg rx rxe rout2 dg cbm cb moe_s gg uu sl fm fh av dd ad whi wlo hh hl "
            "qp qs qss qsd qn qr qd vt vtc f1 f1c f2 f2c sc nmx ex pn tr trc pv pvc ysq2 yss ysd ybd gp pj gsg gt wo2 "
            "xw dve_step act_step outd").split():
            sems[name] = ctx.enter_context(nc.semaphore("s_" + name))
        for g in range(2):
            for name in ("ao", "x1", "x1c", "tb", "tu"):
                sems[f"{name}{g}"] = ctx.enter_context(nc.semaphore(f"s_{name}{g}"))
        ld = [ctx.enter_context(nc.semaphore(f"s_slab{i}")) for i in range(NSLOT)]

        def slab(n):
            return ring[:, (n % NSLOT) * SLAB:(n % NSLOT + 1) * SLAB]

        def whi_of(rel):
            return whi[:, (rel % 3) * SLAB:(rel % 3 + 1) * SLAB]

        def wlo_of(n):
            return wlo[:, (n % NSLOT) * SLAB:(n % NSLOT + 1) * SLAB]

        def slab_wait(eng, n, i=None, turns=0):
            value = 16 * (n // NSLOT + 1)
            eng.wait_ge(ld[n % NSLOT], value if i is None else i * (16 * turns) + value)

        def wait_at(eng, s, base, i=None, step=0):
            if i is None:
                if base > 0:
                    eng.wait_ge(s, base)
            else:
                assert base > 0
                eng.wait_ge(s, i * step + base)

        PH = []
        pairs = drains = splits = 0
        for which in range(5):
            T = [TX, T2, T2, T2, TX][which]
            nb = B_MOE if which == 0 else B_FFN
            s0 = [S_MOE, S_LAYER + L_FFN0, S_LAYER + L_FFN1,
                  S_LAYER + N_LAYER + L_FFN0, S_LAYER + N_LAYER + L_FFN1][which]
            nd = 8 * T // T2
            pre, un = 2, 6 if which == 0 else 3
            PH.append(dict(s0=s0, hn=8 * [0, 1, 3, 4, 6][which], T=T, nb=nb, q0=pairs, m0=drains, w0=splits, h0=KT * which, nd=nd, moe=which == 0,
                           pre=pre, unroll=un, turns=(nb - pre - 1) // un))
            pairs += 2 * nb
            drains += nd * nb
            splits += 3 * nb

        def gate_slab(b):
            return max(3 * b - 1, 0)

        def down_slab(ph, b):
            return 3 * b + 4 if b < ph["nb"] - 1 else 3 * b + 2

        def ffn_walk(ph, loop, step):
            pre, un, turns = ph["pre"], ph["unroll"], ph["turns"]
            for b in range(pre):
                step(b, None)
            with loop(0, turns) as i:
                for b in range(pre, pre + un):
                    step(b, i)
            for b in range(pre + un * turns, ph["nb"]):
                step(b, None)

        QB = (0, 1, 7)

        def jobs(l):
            nq = T2 // P if l == 0 else TX // P
            return [(k, j, q) for k in "ab" for j in range(4) for q in range(nq)]

        def qk_tiles(l):
            tq = T2 if l == 0 else TX
            return ([(j, j // 2, j % 2, tq, 0) for j in range(4)] + [(4, 2, 0, T2, 1)]
                    + [(5 + j, 3 + j // 2, j % 2, tq, 2) for j in range(4)]
                    + [(9 + j, 5 + j // 2, j % 2, T2, 3) for j in range(4)])

        block = ctx.enter_context(nc.Block())

        @block.sync
        def _(sp):
            sp.dma_start(xt_[:, :].rearrange("p (k t) -> p k t", k=KT)[:, :, 0:TX], xT).then_inc(sem("xin"), 16)
            for n in range(NSLOT):
                if n == 2:
                    sp.wait_ge(sem("consts"), 64)
                sp.dma_start(slab(n), slabs[n]).then_inc(ld[n], 16)
            full = NSLABS // NSLOT - 1
            with sp.Fori(0, full) as i:
                for j in range(NSLOT):
                    sp.wait_ge(sem("slab_used"), i * NSLOT + (j + 1))
                    sp.dma_start(slab(j), slabs[bass.ds(i * NSLOT + (NSLOT + j), 1)].rearrange("a p n -> (a p) n")
                                 ).then_inc(ld[j], 16)
            for n in range(NSLOT * (full + 1), NSLABS):
                sp.wait_ge(sem("slab_used"), n - NSLOT + 1)
                sp.dma_start(slab(n), slabs[n]).then_inc(ld[n % NSLOT], 16)

        @block.gpsimd
        def _(pool):
            pool.dma_start(par[:, :], small).then_inc(sem("consts"), 16)
            pool.dma_start(keep[:, :], keepc).then_inc(sem("consts"), 16)
            pool.dma_start(wk[:, 0:NMP], mixp).then_inc(sem("consts"), 16)
            pool.dma_start(cst[:, 0:NCST].bitcast(U16), maskc).then_inc(sem("consts"), 16)
            pool.wait_ge(sem("consts"), 64)
            for u in range(4):
                d = u // 2
                for lv in range(7):
                    for g in range(2):
                        if lv == 0:
                            pool.wait_ge(sem("matc"), 8 * u + 4 * g + 4)
                        else:
                            pool.wait_ge(sem(f"x1{g}"), 7 * u + lv)
                            if lv == 1:
                                pool.wait_ge(sem(f"tu{g}"), 7 * u + 1)
                        pool.tensor_tensor(AO[g], MT[:, 4 * g:4 * g + 4, 0:P],
                                           LEVEL[:, d, lv:lv + 1, :].to_broadcast([P, 4, P]), ALU.mult
                                           ).then_inc(sem(f"ao{g}"), 1)
            pool.wait_ge(sem("rout2"), 1)
            pool.dma_start(XT[:, :, TX:T2], ctxT).then_inc(sem("ctxin"), 16)
            pool.dma_start(cst[:, 0:NCA], attc).then_inc(sem("attin"), 16)
            pool.wait_ge(sem("xr"), 9)
            pool.dma_start(out, XT[:, :, 0:TX]).then_inc(sem("outd"), 16)
            pool.wait_ge(sem("outd"), 16)

        @block.tensor
        def _(pe):
            owed = [0]

            def used(n):
                owed[0] += n

            def group(o, pairs, signal=None):
                last = None
                for k, (a, b) in enumerate(pairs):
                    last = pe.matmul(o, a, b, start=k == 0, stop=k == len(pairs) - 1)
                    if k == 0 and owed[0] and len(pairs) > 1:
                        last.then_inc(sem("slab_used"), owed[0])
                        owed[0] = 0
                if signal is not None:
                    last.then_inc(sem(signal), 1)

            def norm(n, T):
                for j in range(KT):
                    pe.wait_ge(sem("sq"), KT * n + j + 1)
                    mm = pe.matmul(bank[7][:, 0:T], O1024, AC[:, j, 0:T], start=j == 0, stop=j == KT - 1)
                mm.then_inc(sem("ss"), 1)

            def w8(n, half):
                s = slab(n).rearrange("p (k c) -> p k c", k=KT)
                return [s[:, k, half * P:(half + 1) * P] for k in range(KT)]

            ada_n = [0]

            def ada_t(n):
                pe.wait_ge(sem("adr"), n + 1)
                for h in range(2):
                    t = pe.transpose(bank[6 + n % 2][:, 256 + 2 * h:258 + 2 * h],
                                     SROW[n % 2][0:2, h * P:(h + 1) * P], IDENT[0:2, 0:2])
                t.then_inc(sem("adt"), 1)

            def ada(k):
                for _ in range(k):
                    n = ada_n[0]
                    if n == 0:
                        pe.wait_ge(sem("silc"), 1)
                    slab_wait(pe, S_ADA + n)
                    wait_at(pe, sem("modc"), n - 1)
                    s = slab(S_ADA + n).rearrange("p (k c) -> p k c", k=KT)
                    group(bank[6 + n % 2][0:2, 0:FB], [(CSIL[:, k, :], s[:, k, :]) for k in range(KT)], "adm")
                    used(1)
                    if n:
                        ada_t(n - 1)
                    if n == N_ADA - 1:
                        ada_t(n)
                    ada_n[0] += 1

            pe.wait_ge(sem("consts"), 64)
            norm(0, TX)
            pe.wait_ge(sem("hn"), 8)
            for n in range(N_WIN):
                slab_wait(pe, S_WIN + n)
                wait_at(pe, sem("projc"), n - 3)
                for half in range(2):
                    group(b3(n % 4, 2)[:, half, :], [(w, HT[:, k, 0:TX]) for k, w in enumerate(w8(S_WIN + n, half))],
                          "proj" if half else None)
                used(1)
            ada(ADA_KK)
            pe.wait_ge(sem("kk"), 1)
            for j in range(4):
                mm = pe.matmul(b3(j // 2, 2)[:, j % 2, :], BO64, SQM[:, j, :], start=True, stop=True)
            mm.then_inc(sem("kks"), 1)
            for tt in range(2):
                for j in range(4):
                    mm = pe.transpose(bank[2 + tt][:, j * P:(j + 1) * P], p_tile(8 + j)[:, tt * P:(tt + 1) * P], IDENT)
            mm.then_inc(sem("vtr"), 1)
            pe.wait_ge(sem("kkd"), 1)
            pe.wait_ge(sem("vtrc"), 1)

            for d in range(2):
                pe.wait_ge(sem("lin"), 1)
                if d:
                    pe.wait_ge(sem("ybc"), 2)
                lo = 64 * d
                for kind, (wname, tile) in enumerate((("w2", 12), ("a2", 13))):
                    for j in range(4):
                        mm = pe.matmul(b3(2 * kind + j // 2, 2)[:, j % 2, :],
                                       mp(wname)[lo:lo + 64, j * P:(j + 1) * P],
                                       p_tile(tile)[lo:lo + 64, :], start=True, stop=True)
                    mm.then_inc(sem("lora"), 1)
                ada(ADA_PREP)
                ts = d
                pe.wait_ge(sem("prep"), d + 1)
                for k, src in enumerate((BT, KH)):
                    for j in range(4):
                        mm = pe.transpose(bank[k][:, j * P:(j + 1) * P], src[:, j, ts * P:(ts + 1) * P], IDENT)
                mm.then_inc(sem("ktr"), 1)
                for step in range(2):
                    u = 2 * d + step
                    tt = ts if step == 0 else 1 - ts
                    tok = slice(tt * P, (tt + 1) * P)
                    for h in range(8):
                        n = 8 * u + h
                        j, lo = h // 2, 64 * (h % 2)
                        hi = lo + 64
                        b = 2 + h % 4
                        if h >= 4:
                            pe.wait_ge(sem("matc"), n - 3)
                        for k, src in enumerate((BT, KH)):
                            mm = pe.matmul(bank[b][:, k * 256:(k + 1) * 256], src[lo:hi, j, tok],
                                           KR[lo:hi, j, tt, :, :], start=True, stop=True)
                        mm.then_inc(sem("mat"), 1)
                    ada(ADA_MAT)
                    pe.wait_ge(sem("matc"), 8 * u + 8)
                    if step == 0:
                        pe.wait_ge(sem("ktrc"), d + 1)
                    for lv in range(7):
                        for g in range(2):
                            pe.wait_ge(sem(f"ao{g}"), 7 * u + lv + 1)
                            if lv:
                                pe.wait_ge(sem(f"tu{g}"), 7 * u + lv)
                            for h in range(4):
                                mm = pe.matmul(bank[3 * g][:, h * P:(h + 1) * P], AO[g][:, h, :],
                                               TI[g][:, h, :] if lv else IDENT, start=True, stop=True)
                            mm.then_inc(sem(f"x1{g}"), 1)
                        if lv:
                            for g in range(2):
                                pe.wait_ge(sem(f"x1c{g}"), 6 * u + lv)
                                if lv < 6:
                                    for h in range(4):
                                        pe.matmul(bank[3 * g + 1][:, h * P:(h + 1) * P], TTI[g][:, h, :],
                                                  X1[g][:, h, :], start=True, stop=True)
                                for h in range(4):
                                    mm = pe.matmul(bank[3 * g + 2][:, h * P:(h + 1) * P], X1[g][:, h, :],
                                                   TTI[g][:, h, :], start=True, stop=True)
                                mm.then_inc(sem(f"tb{g}"), 1)
                        if lv:
                            ada(1)
                    for g in range(2):
                        pe.wait_ge(sem(f"tu{g}"), 7 * u + 7)
                    if step:
                        pe.wait_ge(sem("stc"), d + 1)
                    for h in range(8):
                        j, lo = h // 2, 64 * (h % 2)
                        terms = [(MT[:, h, 256:384], VT[:, tt, h * HD:(h + 1) * HD])]
                        if step:
                            terms.append((KR[lo:lo + 64, j, tt, 0, :], ST[lo:lo + 64, j, :]))
                        group(bank[2 * (h % 2)][:, j * HD:(j + 1) * HD], terms, "w1" if h == 7 else None)
                    pe.wait_ge(sem("w1c"), u + 1)
                    for h in range(8):
                        mm = pe.matmul(bank[1][:, h * HD:(h + 1) * HD], TTI[h // 4][:, h % 4, :],
                                       W1[:, h * HD:(h + 1) * HD], start=True, stop=True)
                    mm.then_inc(sem("sa"), 1)
                    pe.wait_ge(sem("sac"), u + 1)
                    if step == 0:
                        for h in range(8):
                            j, lo = h // 2, 64 * (h % 2)
                            hs = slice(h * HD, (h + 1) * HD)
                            group(bank[4][lo:lo + 64, j * HD:(j + 1) * HD],
                                  [(BTK[:, hs], SA[:, hs]), (KHK[:, hs], VT[:, tt, hs])],
                                  "stp" if h == 7 else None)
                    for h in range(8):
                        j, lo = h // 2, 64 * (h % 2)
                        hs = slice(h * HD, (h + 1) * HD)
                        terms = [(VT[:, tt, hs], MT[:, h, 384:512]), (SA[:, hs], MT[:, h, P:256])]
                        if step:
                            terms.append((ST[lo:lo + 64, j, :], KR[lo:lo + 64, j, tt, 1, :]))
                        group(bank[5][lo:lo + 64, j * P:(j + 1) * P], terms, "yb" if h == 7 else None)
                    if step == 0:
                        pe.wait_ge(sem("ybc"), u + 1)

            for d in range(2):
                for j in range(2):
                    mm = pe.matmul(b3(d, 2)[:, j, :], mp("gw2")[32 * d:32 * d + 16, j * P:(j + 1) * P],
                                   p_tile(19)[32 * d:32 * d + 16, :], start=True, stop=True)
            mm.then_inc(sem("gu_"), 1)
            pe.wait_ge(sem("ybc"), 4)
            for tt in range(2):
                for h in range(4):
                    mm = pe.transpose(bank[2 + tt][:, h * P:(h + 1) * P], GV[:, h, tt * P:(tt + 1) * P], IDENT)
            mm.then_inc(sem("gtr"), 1)
            ada(ADA_GLA)
            pe.wait_ge(sem("gprep"), 1)
            for d in range(2):
                for j in range(2):
                    mm = pe.transpose(b3(4, 4)[:, 2 * d + j, :], KG[:, 2 * d + j, d * P:(d + 1) * P], IDENT)
            mm.then_inc(sem("gtr"), 1)
            pe.wait_ge(sem("gtrc"), 1)
            for d in range(2):
                for par in range(2):
                    lo = 64 * par
                    for tt in range(2):
                        for j in range(2):
                            tok = slice(tt * P, (tt + 1) * P)
                            mm = pe.matmul(b3(2 * d + par, 4)[:, 2 * tt + j, :], KG[lo:lo + 64, 2 * d + j, tok],
                                           QH[lo:lo + 64, 2 * d + j, tok], start=True, stop=True)
                    mm.then_inc(sem("gmat"), 1)
            pe.wait_ge(sem("gtrc"), 2)
            for d in range(2):
                for h in range(4):
                    lo = 64 * (h % 2)
                    mm = pe.matmul(b3(5, 4)[lo:lo + 64, 2 * d + h // 2, :], KGT[:, d, h // 2, lo:lo + 64],
                                   VG[:, d, h * P:(h + 1) * P], start=True, stop=True)
            mm.then_inc(sem("gst"), 1)
            ada(ADA_GMAT)
            pe.wait_ge(sem("gmatc"), 4)
            pe.wait_ge(sem("gstc"), 1)
            for par in range(2):
                for tt in range(2):
                    d = 1 - tt
                    for j in range(2):
                        lo, h = 64 * par, 2 * j + par
                        tok = slice(tt * P, (tt + 1) * P)
                        vh = VG[:, tt, h * P:(h + 1) * P]
                        group(b3(par, 4)[:, 2 * tt + j, :],
                              [(vh, DT[:, 0, tt, h, :]), (vh, DT[:, 1, tt, h, :]),
                               (STG[lo:lo + 64, d, j, :], QH[lo:lo + 64, 2 * d + j, tok])],
                              "go" if tt == j == 1 else None)

            pe.wait_ge(sem("goc"), 2)
            for j in range(4):
                mm = pe.matmul(b3(j // 2, 2)[:, j % 2, :], BO64, YT[:, j, :], start=True, stop=True)
            mm.then_inc(sem("ym"), 1)
            pe.wait_ge(sem("ysq"), 1)
            for j in range(4):
                mm = pe.matmul(b3(2 + j // 2, 2)[:, j % 2, :], BO64, SQM[:, j, :], start=True, stop=True)
            mm.then_inc(sem("yv"), 1)
            pe.wait_ge(sem("ybon"), 1)
            for j in range(4):
                mm = pe.matmul(b3(j // 2, 2)[:, j % 2, :], BO64, TB[:, j, :], start=True, stop=True)
            mm.then_inc(sem("ybc2"), 1)
            for j in range(4):
                mm = pe.matmul(b3(4 + j // 2, 2)[:, j % 2, :], mp("g2")[:, j * P:(j + 1) * P], p_tile(14),
                               start=True, stop=True)
            mm.then_inc(sem("yg"), 1)
            pe.wait_ge(sem("gsq"), 1)
            for j in range(4):
                mm = pe.matmul(b3(2 + j // 2, 2)[:, j % 2, :], O128, SQM[:, j, :], start=True, stop=True)
            mm.then_inc(sem("gss"), 1)
            ada(N_ADA - ada_n[0])
            pe.wait_ge(sem("mixr"), 1)
            for n in range(4):
                slab_wait(pe, S_WOUT + n)
                for half in range(2):
                    group(b3(n, 2)[:, half, :], [(w, MIX[:, k, :]) for k, w in enumerate(w8(S_WOUT + n, half))],
                          "wo" if half else None)
                used(1)

            norm(1, TX)
            pe.wait_ge(sem("hn"), 16)
            router = mp("router").rearrange("p (k n) -> p k n", k=KT)
            for tt in range(2):
                group(bank[tt][:, 0:36], [(HT[:, k, tt * P:(tt + 1) * P], router[:, k, :]) for k in range(KT)],
                      "lg" if tt else None)
            pe.wait_ge(sem("rout2"), 1)

            def ffn(ph):
                T, s0, q0, m0, w0, nd = ph["T"], ph["s0"], ph["q0"], ph["m0"], ph["w0"], ph["nd"]
                un = ph["unroll"]

                def expert(e, i):
                    wait_at(pe, sem("dg"), e + 1, i, un // 2)
                    wait_at(pe, sem("fm"), q0 + 4 * e, i, 2 * un)
                    for tt in range(2):
                        mm = pe.matmul(bank[3][:, TX + tt * P:TX + (tt + 1) * P], O1024, DG[:, tt, :], start=True, stop=True)
                    mm.then_inc(sem("cbm"), 1)

                def halves(rel, k, c0, parts):
                    c = slice(c0, c0 + P)
                    return (whi_of(rel).rearrange("p (k c) -> p k c", k=parts)[:, k, c],
                            wlo_of(s0 + rel).rearrange("p (k c) -> p k c", k=parts)[:, k, c])

                def first_layer(b, i, rel, bank0, read, signal):
                    wait_at(pe, sem("wlo"), w0 + rel + 1, i, 3 * un)
                    for ft in range(FT):
                        wait_at(pe, sem(read), q0 + 2 * b + ft - 1, i, 2 * un)
                        if ph["moe"] and b % 2 == 0 and bank0 + ft == 3:
                            wait_at(pe, sem("cb"), b // 2 + 1, i, un // 2)
                        pairs3 = []
                        for k in range(KT):
                            hi, lo = halves(rel, k, ft * P, KT)
                            pairs3 += [(hi, HHI[:, k, 0:T]), (hi, HLO[:, k, 0:T]), (lo, HHI[:, k, 0:T])]
                        group(bank[bank0 + ft][:, 0:T], pairs3, signal)
                    used(1)

                def down(b, i):
                    rel = down_slab(ph, b)
                    wait_at(pe, sem("wlo"), w0 + rel + 1, i, 3 * un)
                    wait_at(pe, sem("av"), q0 + 2 * b + 2, i, 2 * un)
                    per = KT // nd
                    for m in range(nd):
                        if b * nd + m >= 4 or i is not None:
                            wait_at(pe, sem("ad"), m0 + b * nd + m - 4 + 1, i, un * nd)
                        for j in range(m * per, (m + 1) * per):
                            pairs3 = []
                            for k in range(FT):
                                hi, lo = halves(rel, k, j * P, FT)
                                fh, fl = FHI[b % 3][:, k, 0:T], FLO[b % 3][:, k, 0:T]
                                pairs3 += [(hi, fh), (hi, fl), (lo, fh)]
                            group(bank[4 + m % 4][:, (j % per) * T:(j % per + 1) * T], pairs3,
                                  "dd" if j % per == per - 1 else None)
                    used(1)

                def step(b, i):
                    if ph["moe"] and b % 2 == 0:
                        expert(b // 2, i)
                    first_layer(b, i, gate_slab(b), 0, "sl", "gg")
                    first_layer(b, i, gate_slab(b) + 1, 2, "fm", "uu")
                    if b or i is not None:
                        down(b - 1, i)

                pe.wait_ge(sem("hl"), ph["h0"] + KT)
                ffn_walk(ph, pe.Fori, step)
                down(ph["nb"] - 1, None)

            ffn(PH[0])
            norm(2, TX)

            for l in range(2):
                tq = T2 if l == 0 else TX
                sl0 = S_LAYER + N_LAYER * l
                norm(3 + 3 * l, T2)
                ffn(PH[1 + 2 * l])
                norm(4 + 3 * l, T2)
                pe.wait_ge(sem("hn"), 16 + 8 * (3 * l + 2))
                pe.wait_ge(sem("lam"), l + 1)
                pe.matmul(bank[7][:, 0:2], BO64, LAMV[:, 0:2], start=True, stop=True).then_inc(sem("lamd"), 1)

                tiles = qk_tiles(l)
                q0 = 13 * l

                def project(i):
                    t, s, half, T, _ = tiles[i]
                    if half == 0:
                        slab_wait(pe, sl0 + L_WIN + s)
                    if i >= 3:
                        pe.wait_ge(sem("qn"), q0 + i - 2)
                    group(bank[QB[i % 3]][:, 0:T], [(w, HT[:, k, 0:T]) for k, w in enumerate(w8(sl0 + L_WIN + s, half))],
                          "qp")
                    if half:
                        used(1)
                    if t == 4:
                        wk8 = w8(sl0 + L_WIN + s, 1)
                        for tt in range(4):
                            group(bank[6][:, tt * P:(tt + 1) * P],
                                  [(HT[:, k, tt * P:(tt + 1) * P], wk8[k]) for k in range(KT)],
                                  "vt" if tt == 3 else None)
                        used(1)

                def square(i):
                    T = tiles[i][3]
                    pe.wait_ge(sem("qs"), q0 + i + 1)
                    pe.matmul(bank[2 + i % 2][:, 0:T], BO64, SQ[i % 2][:, 0:T], start=True, stop=True
                              ).then_inc(sem("qss"), 1)

                def rotate(i):
                    pe.wait_ge(sem("qn"), q0 + i + 1)
                    if i >= 2:
                        pe.wait_ge(sem("qd"), q0 + i - 1)
                    pe.matmul(bank[4 + i % 2][:, 0:TX], ROT, QK[:, tiles[i][0], 0:TX], start=True, stop=True
                              ).then_inc(sem("qr"), 1)

                for i in range(15):
                    if i < 13:
                        project(i)
                    if 1 <= i < 14:
                        square(i - 1)
                    if i >= 2:
                        rotate(i - 2)
                nv = 9 if l == 0 else 7
                v0 = 9 * l
                ev = 1
                for name, s in (("vb", 7), ("uc", 9)):
                    nt = 4 if name == "vb" else tq // P
                    for ss in range(2):
                        slab_wait(pe, sl0 + L_WIN + s + ss)
                        w = slab(sl0 + L_WIN + s + ss).rearrange("p (k c) -> p k c", k=KT)
                        for tp in range(nt // 2):
                            if ev >= 2:
                                pe.wait_ge(sem("vtc"), v0 + ev - 1)
                            for tt in (2 * tp, 2 * tp + 1):
                                group(b3(6 + ev % 2, 2)[:, tt % 2, :],
                                      [(HT[:, k, tt * P:(tt + 1) * P], w[:, k, :]) for k in range(KT)],
                                      "vt" if tt % 2 else None)
                            ev += 1
                        used(1)
                assert ev == nv
                pe.wait_ge(sem("vtc"), v0 + nv)

                nu = 4 * (tq // TX)
                f0 = 8 * l

                def four2(n):
                    pe.wait_ge(sem("f1c"), f0 + n + 1)
                    if n >= 2:
                        pe.wait_ge(sem("f2c"), f0 + n - 1)
                    group(bank[2 + n % 2][:, 0:TX], [(ca["c128"], FTM[n % 2][:, 0:TX]),
                                                     (ca["s128"], FTM[n % 2][:, TX:T2])], "f2")

                pe.wait_ge(sem("qd"), q0 + 13)
                for n in range(nu):
                    g, part = n % 4, n // 4
                    if n >= 2:
                        pe.wait_ge(sem("f1c"), f0 + n - 1)
                    group(bank[n % 2][:, :], [(UC[:, 2 * part + t, g * P:(g + 1) * P], CS[:, t, :]) for t in range(2)],
                          "f1")
                    if n:
                        four2(n - 1)
                four2(nu - 1)
                pe.wait_ge(sem("f2c"), f0 + nu)

                js = jobs(l)
                j0 = 32 * l

                def scores(n):
                    kind, j, q = js[n]
                    if n >= 2:
                        pe.wait_ge(sem("ex"), 2 * (j0 + n - 1))
                    for m in range(2):
                        lo = 64 * m
                        k0 = 0 if q < 2 else TX
                        qt, kt = (j, 4) if kind == "a" else (5 + j, 9 + j)
                        mm = pe.matmul(bank[2 * (n % 2) + m][:, k0:T2], QK[lo:lo + 64, qt, q * P:(q + 1) * P],
                                       QK[lo:lo + 64, kt, k0:T2], start=True, stop=True)
                        mm.then_inc(sem("sc"), 1)

                tr0 = 48 * l

                def tr_index(n):
                    na = min(n, len(js) // 2)
                    return tr0 + 2 * na + (n - na)

                def turns_of(n):
                    kind, j, q = js[n]
                    pe.wait_ge(sem("pn"), j0 + n + 1)
                    for m in range(2 if kind == "a" else 1):
                        x = tr_index(n) + m
                        if x >= 2:
                            pe.wait_ge(sem("trc"), x - 1)
                        for kt in range(0 if q < 2 else 2, 4):
                            t = pe.transpose(bank[4 + x % 2][:, kt * P:(kt + 1) * P],
                                             PR[n % 2][m][:, kt * P:(kt + 1) * P], IDENT)
                        t.then_inc(sem("tr"), 1)

                def values(n):
                    kind, j, q = js[n]
                    if n >= 2:
                        pe.wait_ge(sem("pvc"), j0 + n - 1)
                    kts = range(0 if q < 2 else 2, 4)
                    for m in range(2 if kind == "a" else 1):
                        pe.wait_ge(sem("trc"), tr_index(n) + m + 1)
                        if kind == "a":
                            group(bank[6 + n % 2][64 * m:64 * m + 64, 0:P],
                                  [(VA[:, kt, 64 * m:64 * m + 64], PTR[n % 2][m][:, kt, :]) for kt in kts],
                                  "pv" if m else None)
                        else:
                            group(bank[6 + n % 2][:, 0:P],
                                  [(VB[:, kt, j * P:(j + 1) * P], PTR[n % 2][0][:, kt, :]) for kt in kts], "pv")

                scores(0)
                for n in range(len(js)):
                    if n + 1 < len(js):
                        scores(n + 1)
                    if n:
                        values(n - 1)
                    turns_of(n)
                values(len(js) - 1)
                for h in range(4):
                    pe.wait_ge(sem("ysq2"), 4 * l + h + 1)
                    if h == 0:
                        pe.wait_ge(sem("pvc"), j0 + len(js))
                    pe.matmul(bank[h][:, 0:tq], O128, SQ[h % 2][:, 0:tq], start=True, stop=True
                              ).then_inc(sem("yss"), 1)
                pe.wait_ge(sem("ybd"), 4 * l + 4)

                g0 = 24 * l
                for br in range(3):
                    for j in range(8):
                        n = 8 * br + j
                        base = sl0 + L_MERGE + 6 * br + 3 * (j // 4)
                        gs, bs = base + (j // 2) % 2, base + 2
                        if j % 2 == 0:
                            slab_wait(pe, gs)
                        if j % 4 == 0:
                            slab_wait(pe, bs)
                        if n >= 2:
                            pe.wait_ge(sem("gt"), g0 + n - 1)
                        group(bank[n % 2][:, 0:tq], [(w, HT[:, k, 0:tq]) for k, w in enumerate(w8(gs, j % 2))], "gp")
                        wb = slab(bs).rearrange("p (k c) -> p k c", k=4)
                        src = [[QK[:, k, 0:tq] for k in range(4)], [QK[:, 5 + k, 0:tq] for k in range(4)],
                               [YC[:, k, 0:tq] for k in range(4)]][br]
                        group(bank[2 + n % 2][:, 0:tq],
                              [(wb[:, k, (j % 4) * P:(j % 4 + 1) * P], src[k]) for k in range(4)], "pj")
                        if j % 4 == 1:
                            used(1)
                        if j % 4 == 3:
                            used(2)
                pe.wait_ge(sem("gt"), g0 + 24)
                for j in range(8):
                    n = sl0 + L_WOUT + j // 2
                    slab_wait(pe, n)
                    if j >= 4:
                        pe.wait_ge(sem("xw"), 7 * l + j - 3)
                    group(bank[4 + j % 4][:, 0:tq], [(w, AC[:, k, 0:tq]) for k, w in enumerate(w8(n, j % 2))], "wo2")
                    if j % 2:
                        used(1)
                norm(5 + 3 * l, tq)
                ffn(PH[2 + 2 * l])


        @block.scalar
        def _(act):
            steps = [0]

            def then(ins):
                steps[0] += 1
                ins.then_inc(sem("act_step"), 1)
                act.wait_ge(sem("act_step"), steps[0])

            def split_slab(ph, rel, i=None):
                n, un = ph["s0"] + rel, ph["unroll"]
                slab_wait(act, n, i, 3 * un // NSLOT)
                wait_at(act, sem("slab_used"), n - 2, i, 3 * un)
                act.activation(whi_of(rel), slab(n), ACT.Copy).then_inc(sem("whi"), 1)

            def norm(n, T, ph=None):
                if ph is not None:
                    split_slab(ph, 0)
                    split_slab(ph, 1)
                if n == 0:
                    act.wait_ge(sem("xin"), 16)
                else:
                    act.wait_ge(sem("xr"), n)
                if n == 3:
                    act.wait_ge(sem("ctxin"), 16)
                for j in range(KT):
                    act.activation(AC[:, j, 0:T], XT[:, j, 0:T], ACT.Square).then_inc(sem("sq"), 1)
                act.wait_ge(sem("ss"), n + 1)
                act.activation(rs[:, 0:T], bank[7][:, 0:T], ACT.Sqrt, bias=pc("eps", 0)).then_inc(sem("sd"), 1)
                if n >= 3:
                    l, k = (n - 3) // 3, (n - 3) % 3
                    for j in range(KT):
                        act.wait_ge(sem("hs"), 8 * (n - 3) + j + 1)
                        for half in range(T // TX):
                            o = HT[:, j, half * TX:(half + 1) * TX]
                            ins = act.activation(o, o, ACT.Identity, bias=MOD[:, l, 24 * k + j, half:half + 1])
                        ins.then_inc(sem("hn"), 1)

            ada_n = [0]

            def ada(k):
                for n in range(ada_n[0], ada_n[0] + k):
                    act.wait_ge(sem("adm"), n + 1)
                    if n >= 2:
                        act.wait_ge(sem("adt"), n - 1)
                    act.activation(SROW[n % 2][0:2, :], bank[6 + n % 2][0:2, 0:FB], ACT.Copy).then_inc(sem("adr"), 1)
                ada_n[0] += k

            act.wait_ge(sem("consts"), 64)
            norm(0, TX)
            act.activation(CSIL[:, :, :].rearrange("p a b -> p (a b)"), pc("c", 0, 16), ACT.Silu).then_inc(sem("silc"), 1)
            for n in range(N_WIN):
                act.wait_ge(sem("proj"), n + 1)
                o = PT_[:, 2 * n:2 * n + 2, :] if n < 10 else XT[:, 2 * n - 20:2 * n - 18, TX:T2]
                act.activation(o, b3(n % 4, 2), ACT.Copy).then_inc(sem("projc"), 1)
            ada(ADA_KK)
            act.wait_ge(sem("shifted"), 1)
            act.activation(p_tile(12), p_tile(12), ACT.Tanh)
            act.activation(p_tile(14), p_tile(14), ACT.Sigmoid).then_inc(sem("lin"), 1)
            act.wait_ge(sem("kk2"), 1)
            act.activation(SQM, SQM, ACT.Sqrt).then_inc(sem("kkq"), 1)
            act.wait_ge(sem("vtr"), 1)
            for tt in range(2):
                ins = act.activation(VT[:, tt, :], bank[2 + tt][:, :], ACT.Copy)
            ins.then_inc(sem("vtrc"), 1)
            for d in range(2):
                for kind, (dst, bias) in enumerate(((SG_, "w0"), (BT, "a0"))):
                    act.wait_ge(sem("lora"), 2 * d + kind + 1)
                    for j in range(4):
                        ins = act.activation(dst[:, j, :], b3(2 * kind + j // 2, 2)[:, j % 2, :], ACT.Sigmoid,
                                             bias=pc(bias, 4 * d + j))
                ins.then_inc(sem("sig"), 1)
                ada(ADA_PREP // 3)
                act.wait_ge(sem("cpre"), d + 1)
                inc, exc, s = (CI_, CX_, -KAPPA) if d == 0 else (CX_, CI_, KAPPA)
                act.activation(C_, inc, ACT.Exp, scale=s)
                act.activation(E2_, exc, ACT.Exp, scale=s)
                act.activation(SG_, inc, ACT.Exp, scale=-s)
                act.activation(CR, CR, ACT.Exp, scale=-KAPPA).then_inc(sem("exps"), 1)
                ada(ADA_PREP - ADA_PREP // 3)
                act.wait_ge(sem("ktr"), d + 1)
                act.activation(BTK, bank[0][:, :], ACT.Copy)
                act.activation(KHK, bank[1][:, :], ACT.Copy).then_inc(sem("ktrc"), 1)
                for step in range(2):
                    u = 2 * d + step
                    ada(ADA_MAT)
                    for lv in range(1, 7):
                        for g in range(2):
                            act.wait_ge(sem(f"x1{g}"), 7 * u + lv + 1)
                            act.activation(X1[g], b3(3 * g, 4), ACT.Copy).then_inc(sem(f"x1c{g}"), 1)
                        ada(1)
                    act.wait_ge(sem("w1"), u + 1)
                    for par in range(2):
                        ins = act.activation(W1.rearrange("p (j a n) -> p j a n", j=4, a=2)[:, :, par, :],
                                             bank[2 * par][:, 0:256].rearrange("p (j n) -> p j n", j=4), ACT.Copy)
                    ins.then_inc(sem("w1c"), 1)
                    act.wait_ge(sem("sa"), u + 1)
                    act.activation(SA, bank[1][:, :], ACT.Copy, scale=-1.0).then_inc(sem("sac"), 1)
            act.wait_ge(sem("gu2"), 1)
            then(act.activation(AB_, U_, ACT.Abs))
            then(act.activation(AB_, AB_, ACT.Exp, scale=-1.0))
            act.activation(AB_, AB_, ACT.Ln, bias=pc("eps", 2)).then_inc(sem("gln"), 1)
            act.wait_ge(sem("gtr"), 1)
            for tt in range(2):
                ins = act.activation(VG[:, tt, :], bank[2 + tt][:, :], ACT.Copy)
            ins.then_inc(sem("gtrc"), 1)
            ada(2)
            act.wait_ge(sem("gpre"), 1)
            act.activation(GE1[:, 0:2, :], GCI_[:, 0:2, :], ACT.Exp, scale=1 / TAU)
            act.activation(GE1[:, 2:4, :], AB_[:, 2:4, :], ACT.Exp, scale=-1 / TAU)
            act.activation(GE3[:, 0:2, :], GCI_[:, 0:2, :], ACT.Exp, scale=-1 / TAU)
            act.activation(GE3[:, 2:4, :], AB_[:, 2:4, :], ACT.Exp, scale=1 / TAU)
            act.activation(CRG, CRG, ACT.Exp, scale=1 / TAU).then_inc(sem("gexp"), 1)
            ada(ADA_GLA - 2)
            act.wait_ge(sem("gtr"), 2)
            act.activation(KGT.rearrange("p a b c -> p (a b c)"), bank[4][:, :], ACT.Copy).then_inc(sem("gtrc"), 1)
            ada(ADA_GMAT)
            for par in range(2):
                act.wait_ge(sem("go"), par + 1)
                for tt in range(2):
                    ins = act.activation(OT[:, par:4:2, tt * P:(tt + 1) * P], b3(par, 4)[:, 2 * tt:2 * tt + 2, :],
                                         ACT.Copy)
                ins.then_inc(sem("goc"), 1)
            act.activation(SIL, GOG, ACT.Silu).then_inc(sem("gsil"), 1)
            act.wait_ge(sem("ymc"), 1)
            act.activation(SQM, CEN, ACT.Square).then_inc(sem("ysq"), 1)
            act.wait_ge(sem("yv"), 1)
            for h in range(2):
                ins = act.activation(RSM[:, 2 * h:2 * h + 2, :], b3(2 + h, 2), ACT.Sqrt, bias=pc("eps", 1))
            ins.then_inc(sem("yvd"), 1)
            act.activation(SQM, OT, ACT.Square).then_inc(sem("gsq"), 1)
            act.wait_ge(sem("gss"), 1)
            for h in range(2):
                ins = act.activation(RSG[:, 2 * h:2 * h + 2, :], b3(2 + h, 2), ACT.Sqrt, bias=pc("eps", 0))
            ins.then_inc(sem("gssd"), 1)
            ada(N_ADA - ada_n[0])
            norm(1, TX, PH[0])
            act.wait_ge(sem("rx"), 1)
            act.activation(RC[0], RC[0], ACT.Exp)
            act.activation(RT[1], RT[1], ACT.Exp).then_inc(sem("rxe"), 1)

            def ffn(ph):
                T, q0, un = ph["T"], ph["q0"], ph["unroll"]

                def silu(b, ft, i):
                    q = q0 + 2 * b + ft
                    wait_at(act, sem("gg"), q + 1, i, 2 * un)
                    wait_at(act, sem("av"), q - 1, i, 2 * un)
                    act.activation(FS[ft][:, 0:T], bank[ft][:, 0:T], ACT.Silu).then_inc(sem("sl"), 1)

                def high(b, ft, i):
                    wait_at(act, sem("fm"), q0 + 2 * b + ft + 1, i, 2 * un)
                    act.activation(FHI[b % 3][:, ft, 0:T], FS[ft][:, 0:T], ACT.Copy).then_inc(sem("fh"), 1)

                def step(b, i):
                    if ph["moe"] and b % 2 == 0:
                        e = b // 2
                        wait_at(act, sem("cbm"), e + 1, i, un // 2)
                        act.activation(CBS[e % 3], bank[3][:, TX:T2], ACT.Copy).then_inc(sem("cb"), 1)
                    silu(b, 0, i)
                    silu(b, 1, i)
                    if b < ph["nb"] - 1:
                        split_slab(ph, gate_slab(b + 1), i)
                    high(b, 0, i)
                    high(b, 1, i)
                    if b < ph["nb"] - 1:
                        split_slab(ph, gate_slab(b + 1) + 1, i)
                    split_slab(ph, down_slab(ph, b), i)

                if ph["moe"]:
                    act.wait_ge(sem("rout2"), 1)
                act.wait_ge(sem("hn"), 16 + ph["hn"])
                for j in range(KT):
                    act.activation(HHI[:, j, 0:T], HT[:, j, 0:T], ACT.Copy).then_inc(sem("hh"), 1)
                ffn_walk(ph, act.Fori, step)

            ffn(PH[0])
            norm(2, TX)
            for l in range(2):
                tq = T2 if l == 0 else TX
                norm(3 + 3 * l, T2, PH[1 + 2 * l])
                ffn(PH[1 + 2 * l])
                norm(4 + 3 * l, T2)
                act.wait_ge(sem("lamd"), l + 1)
                act.activation(LAME, bank[7][:, 0:2], ACT.Exp, scale=64.0).then_inc(sem("lame"), 1)
                tiles = qk_tiles(l)
                q0, v0 = 13 * l, 9 * l
                for i in range(14):
                    if i < 13:
                        T = tiles[i][3]
                        act.wait_ge(sem("qp"), q0 + i + 1)
                        wait_at(act, sem("qss"), q0 + i - 1)
                        act.activation(SQ[i % 2][:, 0:T], bank[QB[i % 3]][:, 0:T], ACT.Square).then_inc(sem("qs"), 1)
                    if i == 4:
                        act.wait_ge(sem("vt"), v0 + 1)
                        act.activation(VA, b3(6, 4), ACT.Copy).then_inc(sem("vtc"), 1)
                    if i >= 1:
                        T = tiles[i - 1][3]
                        act.wait_ge(sem("qss"), q0 + i)
                        wait_at(act, sem("qn"), q0 + i - 2)
                        act.activation(RQ[(i - 1) % 2][:, 0:T], bank[2 + (i - 1) % 2][:, 0:T], ACT.Sqrt,
                                       bias=pc("eps", 0)).then_inc(sem("qsd"), 1)
                ev = 1
                for dst, nt in ((VB, 4), (UC, tq // P)):
                    for ss in range(2):
                        for tp in range(nt // 2):
                            act.wait_ge(sem("vt"), v0 + ev + 1)
                            act.activation(dst[:, 2 * tp:2 * tp + 2, ss * TX:(ss + 1) * TX], b3(6 + ev % 2, 2), ACT.Copy
                                           ).then_inc(sem("vtc"), 1)
                            ev += 1
                f0 = 8 * l
                for n in range(4 * (tq // TX)):
                    act.wait_ge(sem("f1"), f0 + n + 1)
                    wait_at(act, sem("f2"), f0 + n - 1)
                    act.activation(FTM[n % 2], bank[n % 2][:, :], ACT.Copy).then_inc(sem("f1c"), 1)
                js = jobs(l)
                j0, tr0 = 32 * l, 48 * l

                def tr_index(n):
                    na = min(n, len(js) // 2)
                    return tr0 + 2 * na + (n - na)

                def exps(n):
                    act.wait_ge(sem("nmx"), j0 + n + 1)
                    if n >= 2:
                        act.wait_ge(sem("tr"), tr_index(n - 1))
                    k0 = 0 if js[n][2] < 2 else TX
                    for m in range(2):
                        c = 2 * (n % 2) + m
                        act.activation(PR[n % 2][m][:, k0:T2], bank[c][:, k0:T2], ACT.Exp, bias=NM[:, c:c + 1],
                                       scale=HD ** -0.5, accum_out=RSUM[:, c:c + 1]).then_inc(sem("ex"), 1)

                exps(0)
                for n in range(len(js)):
                    if n + 1 < len(js):
                        exps(n + 1)
                    kt0 = 0 if js[n][2] < 2 else 2
                    for m in range(2 if js[n][0] == "a" else 1):
                        x = tr_index(n) + m
                        act.wait_ge(sem("tr"), x + 1)
                        if n >= 2:
                            act.wait_ge(sem("pv"), j0 + n - 1)
                        act.activation(PTR[n % 2][m][:, kt0:4, :], b3(4 + x % 2, 4)[:, kt0:4, :], ACT.Copy
                                       ).then_inc(sem("trc"), 1)
                act.wait_ge(sem("pvc"), j0 + len(js))
                for h in range(5):
                    if h < 4:
                        wait_at(act, sem("yss"), 4 * l + h - 1)
                        act.activation(SQ[h % 2][:, 0:tq], QK[:, 5 + h, 0:tq], ACT.Square).then_inc(sem("ysq2"), 1)
                    if h:
                        act.wait_ge(sem("yss"), 4 * l + h)
                        wait_at(act, sem("ybd"), 4 * l + h - 2)
                        act.activation(RQ[(h - 1) % 2][:, 0:tq], bank[h - 1][:, 0:tq], ACT.Sqrt, bias=pc("eps", 0)
                                       ).then_inc(sem("ysd"), 1)
                g0 = 24 * l
                for n in range(24):
                    act.wait_ge(sem("gp"), g0 + n + 1)
                    wait_at(act, sem("gt"), g0 + n - 1)
                    act.activation(GS[n % 2][:, 0:tq], bank[n % 2][:, 0:tq], ACT.Sigmoid).then_inc(sem("gsg"), 1)
                norm(5 + 3 * l, tq, PH[2 + 2 * l])
                ffn(PH[2 + 2 * l])

        @block.vector
        def _(dve):
            steps = [0]

            def then(ins):
                steps[0] += 1
                ins.then_inc(sem("dve_step"), 1)
                dve.wait_ge(sem("dve_step"), steps[0])

            tt_, ts_, stt = dve.tensor_tensor, dve.tensor_scalar, dve.scalar_tensor_tensor

            def split_slab(ph, rel, i=None):
                n, un = ph["s0"] + rel, ph["unroll"]
                wait_at(dve, sem("whi"), ph["w0"] + rel + 1, i, 3 * un)
                slab_wait(dve, n, i, 3 * un // NSLOT)
                tt_(wlo_of(n), slab(n), whi_of(rel).bitcast(F32), ALU.subtract).then_inc(sem("wlo"), 1)

            def norm(n, T, ph=None):
                if n >= 3:
                    l, k = (n - 3) // 3, (n - 3) % 3
                    then(ts_(AMOD, MOD[:, l, 24 * k + 8:24 * k + 16, :], 1.0, None, ALU.add))
                    w = pc("ng", 24 * l + 8 * k, 8).rearrange("p (a b) -> p a b", b=1)
                    then(tt_(AMOD, AMOD, w.to_broadcast([P, 8, 2]), ALU.mult))
                if ph is not None:
                    split_slab(ph, 0)
                    split_slab(ph, 1)
                dve.wait_ge(sem("sd"), n + 1)
                then(dve.reciprocal(rs[:, 0:T], rs[:, 0:T]))
                for j in range(KT):
                    for half in range(T // TX):
                        c = slice(half * TX, (half + 1) * TX)
                        w = AMOD[:, j, half:half + 1] if n >= 3 else pc(("ln1", "ln2", "lnf")[n], j)
                        ins = stt(XT[:, j, c] if n == 2 else HT[:, j, c], XT[:, j, c], w, rs[:, c], ALU.mult, ALU.mult)
                    if n >= 3:
                        ins.then_inc(sem("hs"), 1)
                if n < 2:
                    ins.then_inc(sem("hn"), 8)
                if n == 2:
                    ins.then_inc(sem("xr"), 1)

            ada_n, ada_due = [0], [0]

            def ada(k):
                ada_due[0] += k
                for n in range(ada_n[0], ada_due[0] - (ada_due[0] < N_ADA)):
                    dve.wait_ge(sem("adt"), n + 1)
                    bias = pc("bada", 2 * n, 2).rearrange("p (a b) -> p a b", b=1)
                    tt_(mods[:, 4 * n:4 * n + 4].rearrange("p (a b) -> p a b", b=2),
                        bank[6 + n % 2][:, 256:260].rearrange("p (a b) -> p a b", b=2),
                        bias.to_broadcast([P, 2, 2]), ALU.add).then_inc(sem("modc"), 1)
                    ada_n[0] += 1

            dve.wait_ge(sem("consts"), 64)
            norm(0, TX)
            dve.wait_ge(sem("projc"), 8)
            PR15 = PT_[:, 0:15, :]
            SH = v3(ac_, 0, 15, TX)
            tt_(SH[:, :, 1:TX - 1], PR15[:, :, 0:TX - 2], PR15[:, :, 2:TX], ALU.add)
            dve.tensor_copy(SH[:, :, 0:1], PR15[:, :, 1:2])
            then(dve.tensor_copy(SH[:, :, TX - 1:TX], PR15[:, :, TX - 2:TX - 1]))
            then(stt(SH, SH, 0.5, PR15, ALU.mult, ALU.subtract))
            mu = pc("mu", 0, 15).rearrange("p (a b) -> p a b", b=1)
            then(tt_(SH, SH, mu.to_broadcast([P, 15, TX]), ALU.mult))
            tt_(PR15, PR15, SH, ALU.add).then_inc(sem("shifted"), 1)
            dve.wait_ge(sem("shifted"), 1)
            for j in range(4):
                ins = ts_(KK[:, j, :], p_tile(4 + j), pc("kk", j), None, ALU.mult)
            then(ins)
            ts_(OMKA, pc("ka", 0, 4), -1.0, 1.0, ALU.mult, ALU.add)
            tt_(SQM, KK, KK, ALU.mult).then_inc(sem("kk"), 1)
            ada(ADA_KK)
            dve.wait_ge(sem("kks"), 1)
            for h in range(2):
                ins = ts_(SQM[:, 2 * h:2 * h + 2, :], b3(h, 2), 64.0, 1e-24, ALU.mult, ALU.max)
            ins.then_inc(sem("kk2"), 1)
            dve.wait_ge(sem("kkq"), 1)
            then(dve.reciprocal(SQM, SQM))
            tt_(KK, KK, SQM, ALU.mult).then_inc(sem("kkd"), 1)
            dve.wait_ge(sem("kkd"), 1)
            dve.wait_ge(sem("projc"), 14)

            def carry(out_, ci, g):
                ci4 = ci.rearrange("p a (t n) -> p a t n", t=2)
                g4 = g.rearrange("p a (t n) -> p a t n", t=2)
                o = out_.rearrange("p (a b) -> p a b", b=1)
                then(tt_(o, ci4[:, :, 0, P - 1:P], g4[:, :, 1, 0:1], ALU.add))
                return tt_(o, o, ci4[:, :, 1, 0:1], ALU.subtract)

            for d in range(2):
                dve.wait_ge(sem("sig"), d + 1)
                then(dve.tensor_tensor_scan(C_.rearrange("p a b -> p (a b)"), RESET,
                                            SG_.rearrange("p a b -> p (a b)"), 0.0, ALU.mult, ALU.add))
                c8 = C_.rearrange("p a (t n) -> p (a t) n", t=2)
                then(tt_(CI_.rearrange("p a (t n) -> p (a t) n", t=2), c8, c8[:, :, 63:64].to_broadcast([P, 8, P]),
                         ALU.subtract))
                tt_(CX_, CI_, SG_, ALU.subtract)
                carry(CR, CI_, SG_).then_inc(sem("cpre"), 1)
                ada(ADA_PREP // 3)
                for j in range(4):
                    ins = ts_(KH[:, j, :], BT[:, j, :], pc("ka", j), OMKA[:, j:j + 1], ALU.mult, ALU.add)
                then(ins)
                tt_(BT, BT, KK, ALU.mult)
                then(tt_(KH, KH, PT_[:, 4:8, :], ALU.mult))
                then(tt_(KDS, KDS, KH, ALU.add) if d else dve.tensor_copy(KDS, KH))
                dve.wait_ge(sem("exps"), d + 1)
                tt_(BT, BT, SG_, ALU.mult)
                tt_(KH, KH, SG_, ALU.mult)
                for c, (src, e) in enumerate(((KK, E2_), (PT_[:, 0:4, :], C_))):
                    ins = tt_(KR[:, :, :, c, :], src.rearrange("p a (t n) -> p a t n", t=2),
                              e.rearrange("p a (t n) -> p a t n", t=2), ALU.mult)
                ins.then_inc(sem("prep"), 1)
                ada(ADA_PREP - ADA_PREP // 3)
                for step in range(2):
                    u = 2 * d + step
                    tt = d if step == 0 else 1 - d
                    for h in range(8):
                        dve.wait_ge(sem("mat"), 8 * u + h + 1)
                        tt_(MT[:, h, :], bank[2 + h % 4][:, :], MASK4[:, d, :], ALU.mult).then_inc(sem("matc"), 1)
                    ada(ADA_MAT)
                    eye = IDENT.rearrange("p (a b) -> p a b", a=1).to_broadcast([P, 4, P])
                    for lv in range(7):
                        for g in range(2):
                            if lv == 0:
                                dve.wait_ge(sem(f"x1{g}"), 7 * u + 1)
                                tt_(TI[g], eye, b3(3 * g, 4), ALU.subtract)
                                tt_(TTI[g], eye, AO[g], ALU.subtract).then_inc(sem(f"tu{g}"), 1)
                            else:
                                dve.wait_ge(sem(f"tb{g}"), 6 * u + lv)
                                if lv < 6:
                                    tt_(TI[g], TI[g], b3(3 * g + 1, 4), ALU.subtract)
                                tt_(TTI[g], TTI[g], b3(3 * g + 2, 4), ALU.subtract).then_inc(sem(f"tu{g}"), 1)
                        if lv:
                            ada(1)
                    if step == 0:
                        dve.wait_ge(sem("stp"), d + 1)
                        tt_(ST, bank[4][:, 0:256].rearrange("p (a b) -> p a b", a=4),
                            CR.rearrange("p (a b) -> p a b", b=1).to_broadcast([P, 4, HD]), ALU.mult
                            ).then_inc(sem("stc"), 1)
                    dve.wait_ge(sem("yb"), u + 1)
                    y = YT[:, :, tt * P:(tt + 1) * P]
                    (tt_(y, y, b3(5, 4), ALU.add) if d else dve.tensor_copy(y, b3(5, 4))).then_inc(sem("ybc"), 1)

            dve.wait_ge(sem("gu_"), 1)
            for d in range(2):
                for j in range(2):
                    ins = ts_(U_[:, 2 * d + j, :], b3(d, 2)[:, j, :], pc("gb", 2 * d + j), None, ALU.add)
            ins.then_inc(sem("gu2"), 1)
            dve.wait_ge(sem("gln"), 1)
            then(stt(U_, U_, 0.0, AB_, ALU.min, ALU.subtract))
            then(dve.tensor_tensor_scan(GC_.rearrange("p a b -> p (a b)"), RESET,
                                        U_.rearrange("p a b -> p (a b)"), 0.0, ALU.mult, ALU.add))
            c8 = GC_.rearrange("p a (t n) -> p (a t) n", t=2)
            then(tt_(GCI_.rearrange("p a (t n) -> p (a t) n", t=2), c8, c8[:, :, 63:64].to_broadcast([P, 8, P]),
                     ALU.subtract))
            tt_(AB_, GCI_, U_, ALU.subtract)
            carry(CRG, GCI_, U_).then_inc(sem("gpre"), 1)
            ada(2)
            dve.wait_ge(sem("gexp"), 1)
            for d in range(2):
                o = slice(2 * d, 2 * d + 2)
                stt(QH[:, o, :], PT_[:, 15:17, :], HD ** -0.5, GE1[:, o, :], ALU.mult, ALU.mult)
                ins = tt_(KG[:, o, :], PT_[:, 17:19, :], GE3[:, o, :], ALU.mult)
            ins.then_inc(sem("gprep"), 1)
            ada(ADA_GLA - 2)
            for n in range(4):
                d, par = n // 2, n % 2
                dve.wait_ge(sem("gmat"), n + 1)
                m = MASK4[:, d, P:2 * P].rearrange("p (a b) -> p a b", a=1).to_broadcast([P, 2, P])
                for tt in range(2):
                    ins = tt_(DT[:, d, tt, par:4:2, :], b3(n, 4)[:, 2 * tt:2 * tt + 2, :], m, ALU.mult)
                ins.then_inc(sem("gmatc"), 1)
            dve.wait_ge(sem("gst"), 1)
            tt_(STG.rearrange("p a b c -> p (a b) c"), b3(5, 4),
                CRG.rearrange("p (a b) -> p a b", b=1).to_broadcast([P, 4, P]), ALU.mult).then_inc(sem("gstc"), 1)
            ada(ADA_GMAT)

            dve.wait_ge(sem("ym"), 1)
            for h in range(2):
                ins = tt_(CEN[:, 2 * h:2 * h + 2, :], YT[:, 2 * h:2 * h + 2, :], b3(h, 2), ALU.subtract)
            ins.then_inc(sem("ymc"), 1)
            then(tt_(TB, PT_[:, 0:4, :], KDS, ALU.mult))
            for j in range(4):
                ins = ts_(TB[:, j, :], TB[:, j, :], pc("rk", j), None, ALU.mult)
            ins.then_inc(sem("ybon"), 1)
            dve.wait_ge(sem("yvd"), 1)
            then(dve.reciprocal(RSM, RSM))
            then(tt_(CEN, CEN, RSM, ALU.mult))
            for j in range(4):
                ins = ts_(CEN[:, j, :], CEN[:, j, :], pc("lnw", j), pc("lnb", j), ALU.mult, ALU.add)
            then(ins)
            dve.wait_ge(sem("ybc2"), 1)
            for h in range(2):
                ins = stt(TB[:, 2 * h:2 * h + 2, :], b3(h, 2), 64.0, PT_[:, 8 + 2 * h:10 + 2 * h, :], ALU.mult, ALU.mult)
            then(ins)
            then(tt_(CEN, CEN, TB, ALU.add))
            dve.wait_ge(sem("yg"), 1)
            for h in range(2):
                tt_(MIX[:, 2 * h:2 * h + 2, :], CEN[:, 2 * h:2 * h + 2, :], b3(4 + h, 2), ALU.mult)
            dve.wait_ge(sem("gssd"), 1)
            dve.wait_ge(sem("gsil"), 1)
            then(dve.reciprocal(RSG, RSG))
            then(tt_(OT, OT, RSG, ALU.mult))
            for h in range(4):
                ins = stt(MIX[:, 4 + h, :], OT[:, h, :], pc("gn", h), SIL[:, h, :], ALU.mult, ALU.mult)
            ins.then_inc(sem("mixr"), 1)
            ada(N_ADA - ada_due[0])
            for n in range(4):
                dve.wait_ge(sem("wo"), n + 1)
                x = XT[:, 2 * n:2 * n + 2, 0:TX]
                ins = tt_(x, x, b3(n, 2), ALU.add)
            ins.then_inc(sem("xr"), 1)
            norm(1, TX, PH[0])

            dve.wait_ge(sem("lg"), 1)
            for tt in range(2):
                ins = tt_(LG[:, tt, :], bank[tt][:, 0:36], pc("rb", 0, 36), ALU.add)
            then(ins)

            def b1(r, n):
                return r.rearrange("p (a b) -> p a b", b=1).to_broadcast([P, 2, n])

            def first(out_, values, best, eq, count):
                n = out_.shape[2]
                then(tt_(eq, values, b1(best, n), ALU.is_equal))
                for tt in range(2):
                    ins = dve.tensor_tensor_scan(count[:, tt, :], RESET[:, 1:1 + n], eq[:, tt, :], 0.0, ALU.mult, ALU.add)
                then(ins)
                then(stt(out_, count, 1.0, eq, ALU.is_equal, ALU.mult))

            coarse, fine = LG[:, :, 0:NG], LG[:, :, NG:NG + NE]
            then(dve.tensor_reduce(R1[0], coarse, AX_X, ALU.max))
            tt_(RC[0], coarse, b1(R1[0], NG), ALU.subtract)
            first(RC[3], coarse, R1[0], RC[1], RC[2])
            then(ts_(RC[3], RC[3], 1.0, 1e30, ALU.subtract, ALU.mult))
            then(tt_(RT[0].rearrange("p t (g e) -> p t g e", g=NG), fine.rearrange("p t (g e) -> p t g e", g=NG),
                     RC[3].rearrange("p t (g e) -> p t g e", e=1).to_broadcast([P, 2, NG, EPG]), ALU.add))
            then(dve.tensor_reduce(R1[1], RT[0], AX_X, ALU.max))
            tt_(RT[1], RT[0], b1(R1[1], NE), ALU.subtract).then_inc(sem("rx"), 1)
            first(RT[5], RT[0], R1[1], RT[3], RT[4])
            then(stt(RT[6], RT[5], -2e30, RT[0], ALU.mult, ALU.add))
            then(dve.tensor_reduce(R1[2], RT[6], AX_X, ALU.max))
            first(RT[7], RT[6], R1[2], RT[3], RT[4])
            then(tt_(RT[5], RT[5], RT[7], ALU.add))
            dve.wait_ge(sem("rxe"), 1)
            then(tt_(RT[1], RT[1], RT[5], ALU.mult))
            dve.tensor_reduce(R1[3], RT[1], AX_X, ALU.add)
            then(dve.tensor_reduce(R1[4], RC[0], AX_X, ALU.add))
            then(tt_(R1[3], R1[3], R1[4], ALU.mult))
            then(dve.reciprocal(R1[3], R1[3]))
            tt_(COMB, RT[1], b1(R1[3], NE), ALU.mult).then_inc(sem("rout2"), 1)
            dve.wait_ge(sem("rout2"), 1)

            def spread(e, i, step):
                for tt in range(2):
                    c = tt * NE + e
                    flat = COMB.rearrange("p a b -> p (a b)")
                    w = flat[:, c:c + 1] if i is None else flat[:, bass.ds(i * step + c, 1)]
                    ins = ts_(DG[:, tt, :], IDENT, w, 1024.0, ALU.mult, ALU.mult)
                ins.then_inc(sem("dg"), 1)

            def ffn(ph):
                T, q0, m0, nd, moe = ph["T"], ph["q0"], ph["m0"], ph["nd"], ph["moe"]
                un = ph["unroll"]

                def product(b, ft, i):
                    q = q0 + 2 * b + ft
                    s = FS[ft][:, 0:T]
                    wait_at(dve, sem("sl"), q + 1, i, 2 * un)
                    if moe:
                        tt_(s, s, CBS[b // 2 % 3], ALU.mult).then_inc(sem("moe_s"), 1)
                        wait_at(dve, sem("moe_s"), 2 * b + ft + 1, i, 2 * un)
                    wait_at(dve, sem("uu"), q + 1, i, 2 * un)
                    tt_(s, s, bank[2 + ft][:, 0:T], ALU.mult).then_inc(sem("fm"), 1)

                def low(b, ft, i):
                    q = q0 + 2 * b + ft
                    wait_at(dve, sem("fh"), q + 1, i, 2 * un)
                    tt_(FLO[b % 3][:, ft, 0:T], FS[ft][:, 0:T], FHI[b % 3][:, ft, 0:T].bitcast(F32), ALU.subtract
                        ).then_inc(sem("av"), 1)

                def down(b, i):
                    for m in range(nd):
                        wait_at(dve, sem("dd"), m0 + b * nd + m + 1, i, nd * un)
                        per = KT // nd
                        o = AC[:, m * per:(m + 1) * per, 0:T]
                        s = b3(4 + m % 4, per)
                        (tt_(o, o, s, ALU.add) if b else dve.tensor_copy(o, s)).then_inc(sem("ad"), 1)

                def step(b, i):
                    if b < ph["nb"] - 1:
                        split_slab(ph, gate_slab(b + 1), i)
                    if moe and b % 2 == 0:
                        e = b // 2
                        if e < NE - 1:
                            wait_at(dve, sem("cbm"), e + 1, i, un // 2)
                            spread(e + 1, i, un // 2)
                        wait_at(dve, sem("cb"), e + 1, i, un // 2)
                    product(b, 0, i)
                    product(b, 1, i)
                    low(b, 0, i)
                    low(b, 1, i)
                    if b or i is not None:
                        down(b - 1, i)
                    if b < ph["nb"] - 1:
                        split_slab(ph, gate_slab(b + 1) + 1, i)
                    split_slab(ph, down_slab(ph, b), i)

                for j in range(KT):
                    dve.wait_ge(sem("hh"), ph["h0"] + j + 1)
                    tt_(HLO[:, j, 0:T], HT[:, j, 0:T], HHI[:, j, 0:T].bitcast(F32), ALU.subtract
                        ).then_inc(sem("hl"), 1)
                if moe:
                    spread(0, None, 0)
                ffn_walk(ph, dve.Fori, step)
                down(ph["nb"] - 1, None)
                dve.wait_ge(sem("ad"), m0 + nd * ph["nb"])

            def add_gated(T, src):
                for half in range(T // TX):
                    c = slice(half * TX, (half + 1) * TX)
                    for j in range(KT):
                        ins = stt(XT[:, j, c], src[:, j, c], GMOD[:, j, half:half + 1], XT[:, j, c], ALU.mult, ALU.add)
                return ins

            ffn(PH[0])
            tt_(XT[:, :, 0:TX], XT[:, :, 0:TX], AC[:, :, 0:TX], ALU.add).then_inc(sem("xr"), 1)
            norm(2, TX)
            dve.wait_ge(sem("attin"), 16)
            for l in range(2):
                tq = T2 if l == 0 else TX
                lam_init = 0.8 - 0.6 * math.exp(-0.3 * l)
                for which, n in ((0, 3 + 3 * l), (1, 4 + 3 * l)):
                    norm(n, T2, PH[1 + 2 * l] if which == 0 else None)
                    if which == 0:
                        ffn(PH[1 + 2 * l])
                        then(ts_(GMOD, MOD[:, l, 16:24, :], 0.5, None, ALU.mult))
                        add_gated(T2, AC).then_inc(sem("xr"), 1)
                lm = pc("lam", 4 * l, 4).rearrange("p (a b) -> p a b", b=2)
                tt_(LAMV[:, 0:2].rearrange("p (a b) -> p a b", b=1), lm[:, :, 0:1], lm[:, :, 1:2], ALU.mult
                    ).then_inc(sem("lam"), 1)
                dve.wait_ge(sem("lame"), l + 1)
                then(tt_(NLAM, LAME[:, 1:2], LAME[:, 0:1], ALU.subtract))
                ts_(NLAM, NLAM, lam_init, None, ALU.subtract)
                ts_(SUBS, pc("sub", l), 1.0 - lam_init, None, ALU.mult)
                tiles = qk_tiles(l)
                q0 = 13 * l
                for i in range(14):
                    if i < 13:
                        t, _, _, T, row = tiles[i]
                        r = RQ[i % 2][:, 0:T]
                        dve.wait_ge(sem("qsd"), q0 + i + 1)
                        then(dve.reciprocal(r, r))
                        stt(QK[:, t, 0:T], bank[QB[i % 3]][:, 0:T], pc("qkg", 4 * l + row), r, ALU.mult, ALU.mult
                            ).then_inc(sem("qn"), 1)
                    if i:
                        t = tiles[i - 1][0]
                        x = QK[:, t, 0:TX]
                        dve.wait_ge(sem("qr"), q0 + i)
                        tt_(RTMP[i % 2], bank[4 + (i - 1) % 2][:, 0:TX], ca["sin"], ALU.mult)
                        then(tt_(x, x, ca["cos"], ALU.mult))
                        tt_(x, x, RTMP[i % 2], ALU.add).then_inc(sem("qd"), 1)
                f0 = 8 * l
                for n in range(4 * (tq // TX)):
                    dve.wait_ge(sem("f2"), f0 + n + 1)
                    dve.tensor_copy(YC[:, n % 4, (n // 4) * TX:(n // 4 + 1) * TX], bank[2 + n % 2][:, 0:TX]
                                    ).then_inc(sem("f2c"), 1)
                js = jobs(l)
                j0 = 32 * l

                def maxima(n):
                    k0 = 0 if js[n][2] < 2 else TX
                    for m in range(2):
                        c = 2 * (n % 2) + m
                        dve.wait_ge(sem("sc"), 2 * (j0 + n) + m + 1)
                        ins = dve.tensor_reduce(NM[:, c:c + 1], bank[c][:, k0:T2], AX_X, ALU.max, negate=True)
                    then(ins)
                    c = slice(2 * (n % 2), 2 * (n % 2) + 2)
                    ts_(NM[:, c], NM[:, c], HD ** -0.5, None, ALU.mult).then_inc(sem("nmx"), 1)

                def scale(n):
                    k0 = 0 if js[n][2] < 2 else TX
                    c = 2 * (n % 2)
                    dve.wait_ge(sem("ex"), 2 * (j0 + n) + 2)
                    then(dve.reciprocal(RREC[:, c:c + 2], RSUM[:, c:c + 2]))
                    p0, p1 = (PR[n % 2][m][:, k0:T2] for m in range(2))
                    if js[n][0] == "a":
                        ts_(p0, p0, RREC[:, c:c + 1], None, ALU.mult)
                        ins = ts_(p1, p1, RREC[:, c + 1:c + 2], None, ALU.mult)
                    else:
                        tt_(RREC[:, c + 1:c + 2], RREC[:, c + 1:c + 2], NLAM, ALU.mult)
                        then(ts_(p0, p0, RREC[:, c:c + 1], None, ALU.mult))
                        ins = stt(p0, p1, RREC[:, c + 1:c + 2], p0, ALU.mult, ALU.add)
                    ins.then_inc(sem("pn"), 1)

                def result(n):
                    kind, j, q = js[n]
                    dve.wait_ge(sem("pv"), j0 + n + 1)
                    dve.tensor_copy(QK[:, j if kind == "a" else 5 + j, q * P:(q + 1) * P], bank[6 + n % 2][:, 0:P]
                                    ).then_inc(sem("pvc"), 1)

                maxima(0)
                for n in range(len(js)):
                    if n + 1 < len(js):
                        maxima(n + 1)
                    scale(n)
                    if n:
                        result(n - 1)
                result(len(js) - 1)
                for h in range(4):
                    dve.wait_ge(sem("ysd"), 4 * l + h + 1)
                    r, x = RQ[h % 2][:, 0:tq], QK[:, 5 + h, 0:tq]
                    then(dve.reciprocal(r, r))
                    stt(x, x, SUBS, r, ALU.mult, ALU.mult).then_inc(sem("ybd"), 1)
                g0 = 24 * l
                for n in range(24):
                    j = n % 8
                    dve.wait_ge(sem("gsg"), g0 + n + 1)
                    dve.wait_ge(sem("pj"), g0 + n + 1)
                    a, b = GS[n % 2][:, 0:tq], bank[2 + n % 2][:, 0:tq]
                    if n < 8:
                        tt_(AC[:, j, 0:tq], a, b, ALU.mult).then_inc(sem("gt"), 1)
                    else:
                        then(tt_(GTMP[n % 2][:, 0:tq], a, b, ALU.mult))
                        tt_(AC[:, j, 0:tq], AC[:, j, 0:tq], GTMP[n % 2][:, 0:tq], ALU.add).then_inc(sem("gt"), 1)
                for j in range(8):
                    dve.wait_ge(sem("wo2"), 8 * l + j + 1)
                    for half in range(tq // TX):
                        c = slice(half * TX, (half + 1) * TX)
                        ins = stt(XT[:, j, c], bank[4 + j % 4][:, c], MOD[:, l, 40 + j, half:half + 1], XT[:, j, c],
                                  ALU.mult, ALU.add)
                    ins.then_inc(sem("xr" if j == 7 else "xw"), 1)
                norm(5 + 3 * l, tq, PH[2 + 2 * l])
                ffn(PH[2 + 2 * l])
                then(ts_(GMOD, MOD[:, l, 64:72, :], 0.5, None, ALU.mult))
                add_gated(tq, AC).then_inc(sem("xr"), 1)


def _cols(w, c0, n):
    out = np.zeros((P, KT, FB), np.float32)
    out[:, :, 0:n] = w[:, c0:c0 + n].reshape(KT, P, n).transpose(1, 0, 2)
    return out.reshape(P, SLAB)


def _rows(w, r0):
    return w[r0:r0 + FB].reshape(FT, P, D).transpose(1, 0, 2).reshape(P, SLAB)


def _chan(v):
    v = np.asarray(v, np.float32)
    return v.reshape(-1, P).T


def _masks():
    s, t = np.meshgrid(np.arange(P), np.arange(P), indexing="ij")
    strict, incl = (s < t) * 1.0, (s <= t) * 1.0
    mask4 = np.stack([np.concatenate([m[0], m[1], m[0], m[1]], 1) for m in ((strict, incl), (strict.T, incl.T))], 1)
    level = []
    for lv in range(7):
        same = (s >> (lv + 1)) == (t >> (lv + 1))
        level.append(same & ((s >> lv) % 2 == 0) & ((t >> lv) % 2 == 1))
    level = np.stack([np.stack([m * 1.0 for m in level], 1), np.stack([m.T * 1.0 for m in level], 1)], 1)
    reset = np.ones((P, 1024))
    reset[:, ::P] = 0
    return np.concatenate([mask4.reshape(P, -1), level.reshape(P, -1), reset], 1).astype(np.uint16) * np.uint16(0x3f80)


def _kept():
    eye = np.eye(P)
    block = np.kron(np.eye(2), np.ones((HD, HD))) / HD
    rot = np.zeros((P, P))
    for h in range(2):
        for i in range(32):
            a, b = 64 * h + i, 64 * h + 32 + i
            rot[b, a] = -1.0
            rot[a, b] = 1.0
    return np.concatenate([eye, np.full((P, P), 1 / D), np.full((P, P), 1 / P), block, rot], 1).astype(np.float32)


def _attention_consts():
    n = np.arange(TX)
    a = 2 * np.pi * (np.outer(n, n) % TX) / TX
    cs = np.concatenate([np.cos(a), np.sin(a)], 1).reshape(2, P, 2 * TX).transpose(1, 0, 2).reshape(P, -1)
    c = np.arange(P)
    b = 2 * np.pi * (np.outer(c, c) % P) / P
    norm = 1 / math.sqrt(TX * P)
    grid_w = 64
    rows = TX // grid_w
    nf = HD // 4
    inv = np.power(np.float32(10000.0), -np.arange(nf, dtype=np.float32) / np.float32(nf)).astype(np.float32)
    row = np.repeat(np.arange(rows, dtype=np.float32), grid_w)
    col = np.tile(np.arange(grid_w, dtype=np.float32), rows)
    ang = np.concatenate([row[:, None] * inv, col[:, None] * inv], -1)
    cos, sin = (np.tile(f(ang).T, (4, 1)) for f in (np.cos, np.sin))
    return np.concatenate([cs, np.cos(b) * norm, -np.sin(b) * norm, cos, sin], 1).astype(np.float32)


def _slabs(g):
    out = np.empty((NSLABS, P, SLAB), np.float32)
    w = g["w_in"][0]
    rw = 3 * RW + 2 * 64 + 2 * 64 + 128
    q, k, v = rw, rw + 256, rw + 512
    gl, og = rw + 1024, rw + 1056
    gates = np.zeros((D, P), np.float32)
    gates[:, 0:16] = w[:, gl:gl + 16]
    gates[:, 32:48] = w[:, gl + 16:gl + 32]
    w = np.concatenate([w[:, 0:rw], w[:, q:q + 256], w[:, k:k + 256], gates, w[:, v:v + 512], w[:, og:og + 512]], 1)
    for n in range(N_WIN):
        out[S_WIN + n] = _cols(w, n * FB, FB)
    for n in range(N_ADA):
        l, c = divmod(n, N_ADA // 2)
        out[S_ADA + n] = _cols(g["w_ada_2"][l], c * FB, FB)
    for n in range(4):
        out[S_WOUT + n] = _cols(g["w_out"][0], n * FB, FB)
    def block_slabs(at, nb, b, gate, up, down):
        first = at + max(3 * b - 1, 0)
        out[first], out[first + 1] = gate, up
        out[at + 3 * b + (4 if b < nb - 1 else 2)] = down

    for b in range(B_MOE):
        e, h = divmod(b, 2)
        block_slabs(S_MOE, B_MOE, b, _cols(g["moe_w_gate"][0, e], h * FB, FB),
                    _cols(g["moe_w_up"][0, e], h * FB, FB), _rows(g["moe_w_down"][0, e], h * FB))
    for l in range(2):
        s = S_LAYER + N_LAYER * l
        for f, at in enumerate((L_FFN0, L_FFN1)):
            wi, wo = g["ffn_wi_2"][l, f], g["ffn_wo_2"][l, f]
            for b in range(B_FFN):
                block_slabs(s + at, B_FFN, b, _cols(wi, b * FB, FB), _cols(wi, DFF + b * FB, FB), _rows(wo, b * FB))
        w = g["w_in_2"][l]
        heads = np.concatenate([np.arange(HD) + HD * h for j in range(4) for h in (j, 4 + j)])
        o = 0
        for c0, cols in ((None, 2), (512, 1), (768, 2), (1280, 2), (1792, 2), (2304, 2)):
            for c in range(cols):
                src = w[:, heads] if c0 is None else w
                out[s + L_WIN + o] = _cols(src, (c0 or 0) + c * FB, FB)
                o += 1
        wb = g["w_branch_2"][l]
        for br in range(3):
            b = wb[br][heads] if br == 0 else wb[br]
            for h in range(2):
                m = s + L_MERGE + 6 * br + 3 * h
                for c in range(2):
                    out[m + c] = _cols(w, 2816 + D * br + (2 * h + c) * FB, FB)
                out[m + 2] = b[:, h * 512:(h + 1) * 512].reshape(4, P, 512).transpose(1, 0, 2).reshape(P, SLAB)
        for n in range(4):
            out[s + L_WOUT + n] = _cols(g["w_out_2"][l], n * FB, FB)
    return out


def _small(g):
    SM, n = places(SMALL)
    out = np.zeros((P, n), np.float32)

    def put(name, v):
        o, k = SM[name]
        out[:, o:o + k] = v

    put("ln1", _chan(g["ln1_w"][0]))
    put("mu", _chan(g["rw_mu"][0]))
    put("w0", np.concatenate([_chan(g["rw_w0_f"][0]), _chan(g["rw_w0_b"][0])], 1))
    put("a0", np.concatenate([_chan(g["rw_a0_f"][0]), _chan(g["rw_a0_b"][0])], 1))
    for name, src in (("kk", "rw_k_k"), ("ka", "rw_k_a"), ("lnw", "rw_ln_w"), ("lnb", "rw_ln_b"),
                      ("gn", "gla_norm_w"), ("ln2", "ln2_w")):
        put(name, _chan(g[src][0]))
    put("rk", _chan(g["rw_r_k"][0].reshape(-1)))
    put("gb", np.concatenate([_chan(g["gla_gb_f"][0]), _chan(g["gla_gb_b"][0])], 1))
    put("lnf", _chan(g["ln_f_w"]))
    put("rb", np.tile(np.concatenate([g["moe_b_coarse"][0], g["moe_b_fine"][0]])[None], (P, 1)))
    put("ng", _chan(g["norm_g_2"]))
    put("qkg", np.tile(g["qk_g_2"].reshape(8, HD).T, (2, 1)))
    put("sub", g["diff_subln_g_2"].T)
    put("lam", np.tile(g["diff_lam_2"].reshape(8, HD).T, (2, 1)))
    put("bada", _chan(g["b_ada_2"]))
    put("c", np.stack([_chan(g["c_2"][0]), _chan(g["c_ctx_2"])], 2).reshape(P, 16))
    put("eps", np.array([[RMS_EPS, GN_EPS, 1.0]]))
    return out


def _mixp(g):
    MP, n = places(MIXP)
    out = np.zeros((P, n), np.float32)
    r = np.concatenate([g["moe_w_coarse"][0], g["moe_w_fine"][0]], 1)
    parts = {
        "router": r.reshape(KT, P, 36).transpose(1, 0, 2).reshape(P, -1),
        "w2": np.concatenate([g["rw_w2_f"][0], g["rw_w2_b"][0]], 0),
        "a2": np.concatenate([g["rw_a2_f"][0], g["rw_a2_b"][0]], 0),
        "g2": g["rw_g2"][0],
    }
    for name, v in parts.items():
        o, k = MP[name]
        out[:, o:o + k] = v
    o, k = MP["gw2"]
    out[0:16, o:o + k] = g["gla_gw2_f"][0]
    out[32:48, o:o + k] = g["gla_gw2_b"][0]
    return out


def _turned(x):
    return np.ascontiguousarray(x[0].reshape(TX, KT, P).transpose(2, 1, 0))


def kernel(**inputs):
    import concourse.bacc as bacc
    from concourse.bass_utils import run_bass_kernel_spmd as run

    g = {k: np.asarray(v) for k, v in inputs.items()}
    arrays = {
        "slabs": _slabs(g), "xT": _turned(g["x"]), "ctxT": _turned(g["ctx_2"]), "small": _small(g),
        "mixp": _mixp(g), "attc": _attention_consts(), "keepc": _kept(), "maskc": _masks(),
    }
    nc = bacc.Bacc("TRN2", target_bir_lowering=False, num_devices=1)
    args = [nc.dram_tensor(n, a.shape, mybir.dt.from_np(a.dtype), kind="ExternalInput").ap() for n, a in arrays.items()]
    args.append(nc.dram_tensor("out", (P, KT, TX), F32, kind="ExternalOutput").ap())
    build(nc, *args)
    r = run(nc, [arrays], core_ids=[0])
    o = np.asarray(r.results[0]["out"])
    return np.ascontiguousarray(o.transpose(2, 1, 0).reshape(1, TX, D))
```
